# Optimizing a Trainium2 kernel written in Bass

```python
import math
import jax, jax.numpy as jnp
from jax import lax
import numpy as np

D_MODEL = 1024
BATCH = 1
SEQ = 256
DEPTH = 2

HEAD_DIM = 64
SWA_HEADS = 6
SWA_KV_HEADS = 2
SWA_WINDOW = 128
SWA_BLOCK = 128
SSD_HEADS = 6
SSD_HEAD_DIM = 64
SSD_D_INNER = SSD_HEADS * SSD_HEAD_DIM
SSD_GROUPS = 2
SSD_STATE = 64
SSD_CONV = 5
SSD_CHUNK = 128
DIFF_HEADS = 4
DIFF_QK_DIM = 32
DIFF_V_DIM = 2 * DIFF_QK_DIM
DIFF_Q_BLOCK = 128
N_ALIBI_HEADS = SWA_HEADS + DIFF_HEADS
A_Q_DIM = SWA_HEADS * HEAD_DIM
A_KV_DIM = SWA_KV_HEADS * HEAD_DIM
SSD_BC_DIM = SSD_GROUPS * SSD_STATE
SSD_CONV_DIM = SSD_D_INNER + 2 * SSD_BC_DIM
SSD_DT_DIM = 2 * SSD_HEADS
DIFF_QK_WIDTH = DIFF_HEADS * 2 * DIFF_QK_DIM
DIFF_V_WIDTH = DIFF_HEADS * DIFF_V_DIM
D_IN = A_Q_DIM + 2 * A_KV_DIM + SSD_D_INNER + SSD_CONV_DIM + SSD_DT_DIM + 2 * DIFF_QK_WIDTH + DIFF_V_WIDTH
D_MIX = A_Q_DIM + SSD_D_INNER + DIFF_V_WIDTH
N_EXPERT_GROUPS = 4
EXPERTS_PER_GROUP = 8
N_EXPERTS = N_EXPERT_GROUPS * EXPERTS_PER_GROUP
EXPERT_TOP_K = 2
D_FF_EXPERT = 512
NORM_EPS = 1e-6

kernel_name = 'hymba_style_hybrid_encoder_hmoe'

def rms_norm(x, w):
    xf = x.astype(jnp.float32)
    y = xf * lax.rsqrt(jnp.mean(xf * xf, axis=-1, keepdims=True) + NORM_EPS)
    return (y * w.astype(jnp.float32)).astype(x.dtype)

def alibi_slopes():
    return jnp.exp2(-8.0 * jnp.arange(1, N_ALIBI_HEADS + 1, dtype=jnp.float32) / N_ALIBI_HEADS)

def windowed_gqa_sink(q, k, v, sink, slopes):
    b, s = q.shape[0], q.shape[1]
    nb = s // SWA_BLOCK
    rep = SWA_HEADS // SWA_KV_HEADS
    f32 = jnp.float32
    qb = q.reshape(b, nb, SWA_BLOCK, SWA_KV_HEADS, rep, HEAD_DIM)
    pad = ((0, 0), (SWA_BLOCK, SWA_BLOCK), (0, 0), (0, 0))
    kp = jnp.pad(k, pad).reshape(b, nb + 2, SWA_BLOCK, SWA_KV_HEADS, HEAD_DIM)
    vp = jnp.pad(v, pad).reshape(b, nb + 2, SWA_BLOCK, SWA_KV_HEADS, HEAD_DIM)
    def band(t):
        return jnp.concatenate([t[:, :-2], t[:, 1:-1], t[:, 2:]], axis=2)
    kb, vb = band(kp), band(vp)
    scores = jnp.einsum('bnqgrd,bnkgd->bngrqk', qb, kb).astype(f32) * (HEAD_DIM ** -0.5)
    qi = jnp.arange(SWA_BLOCK)[:, None]
    kj = jnp.arange(3 * SWA_BLOCK)[None, :]
    rel = qi - kj + SWA_BLOCK
    kpos = jnp.arange(nb)[:, None] * SWA_BLOCK - SWA_BLOCK + jnp.arange(3 * SWA_BLOCK)[None, :]
    valid = (jnp.abs(rel) <= SWA_WINDOW)[None] & ((kpos >= 0) & (kpos < s))[:, None, :]
    bias = -slopes.astype(f32).reshape(SWA_KV_HEADS, rep)[:, :, None, None] * jnp.abs(rel).astype(f32)
    scores = jnp.where(valid[None, :, None, None], scores + bias[None, None], -jnp.inf)
    sink_l = sink.astype(f32).reshape(1, 1, SWA_KV_HEADS, rep, 1, 1)
    m = jnp.maximum(jnp.max(scores, axis=-1, keepdims=True), sink_l)
    p = jnp.exp(scores - m)
    denom = jnp.sum(p, axis=-1, keepdims=True) + jnp.exp(sink_l - m)
    probs = (p / denom).astype(v.dtype)
    out = jnp.einsum('bngrqk,bnkgd->bnqgrd', probs, vb)
    return out.reshape(b, s, SWA_HEADS * HEAD_DIM)

def diff_attention(q, k, v, lam_params, subln_w, slopes, lambda_init):
    b, s = q.shape[0], q.shape[1]
    nb = s // DIFF_Q_BLOCK
    f32 = jnp.float32
    lp = lam_params.astype(f32)
    lam = jnp.exp(jnp.sum(lp[0] * lp[1])) - jnp.exp(jnp.sum(lp[2] * lp[3])) + lambda_init
    qb = jnp.moveaxis(q.reshape(b, nb, DIFF_Q_BLOCK, DIFF_HEADS, 2, DIFF_QK_DIM), 1, 0)
    kpos = jnp.arange(s)
    sl = slopes.astype(f32)[None, :, None, None, None]
    def block(args):
        n, qn = args
        sc = jnp.einsum('bqhmd,bkhmd->bhmqk', qn, k).astype(f32) * (DIFF_QK_DIM ** -0.5)
        qpos = n * DIFF_Q_BLOCK + jnp.arange(DIFF_Q_BLOCK)
        dist = jnp.abs(qpos[:, None] - kpos[None, :]).astype(f32)
        a = jax.nn.softmax(sc - sl * dist, axis=-1)
        attn = (a[:, :, 0] - lam * a[:, :, 1]).astype(v.dtype)
        return jnp.einsum('bhqk,bkhd->bqhd', attn, v)
    out = lax.map(block, (jnp.arange(nb), qb))
    out = jnp.moveaxis(out, 0, 1).reshape(b, s, DIFF_HEADS, DIFF_V_DIM)
    out = rms_norm(out, subln_w) * (1.0 - lambda_init)
    return out.reshape(b, s, DIFF_HEADS * DIFF_V_DIM)

def ssd_chunked(x, dt, a, bm, cm):
    b, s, h, p = x.shape
    nc = s // SSD_CHUNK
    rep = h // SSD_GROUPS
    f32 = jnp.float32
    xdt = (x.astype(f32) * dt[..., None]).reshape(b, nc, SSD_CHUNK, h, p)
    da = jnp.cumsum((dt * a).reshape(b, nc, SSD_CHUNK, h), axis=2)
    bh = jnp.repeat(bm.astype(f32), rep, axis=2).reshape(b, nc, SSD_CHUNK, h, SSD_STATE)
    ch = jnp.repeat(cm.astype(f32), rep, axis=2).reshape(b, nc, SSD_CHUNK, h, SSD_STATE)
    lower = jnp.tril(jnp.ones((SSD_CHUNK, SSD_CHUNK), dtype=bool))[None, None, :, :, None]
    seg = da[:, :, :, None, :] - da[:, :, None, :, :]
    decay = jnp.exp(jnp.where(lower, seg, -jnp.inf))
    y_diag = jnp.einsum('bclsh,bcshp->bclhp', jnp.einsum('bclhn,bcshn->bclsh', ch, bh) * decay, xdt)
    to_end = jnp.exp(da[:, :, -1:, :] - da)
    states = jnp.einsum('bclhn,bclhp->bchpn', bh * to_end[..., None], xdt)
    chunk_decay = jnp.exp(da[:, :, -1, :])
    def step(carry, inp):
        st, dec = inp
        return carry * dec[:, :, None, None] + st, carry
    init = jnp.zeros((b, h, p, SSD_STATE), f32)
    _, prev = lax.scan(step, init, (jnp.moveaxis(states, 1, 0), jnp.moveaxis(chunk_decay, 1, 0)))
    prev = jnp.moveaxis(prev, 0, 1)
    y_off = jnp.einsum('bclhn,bchpn->bclhp', ch * jnp.exp(da)[..., None], prev)
    return (y_diag + y_off).reshape(b, s, h, p).astype(x.dtype)

def ssd_mixer(z, xbc, dt_raw, conv_w, conv_b, dt_bias, a_log, d_skip, norm_w):
    b, s = z.shape[0], z.shape[1]
    f32 = jnp.float32
    half = SSD_CONV // 2
    xbc = lax.conv_general_dilated(xbc, conv_w[:, None, :], window_strides=(1,), padding=[(half, half)],
                                   dimension_numbers=('NWC', 'WIO', 'NWC'), feature_group_count=SSD_CONV_DIM)
    xbc = jax.nn.silu(xbc + conv_b)
    xs, bm, cm = jnp.split(xbc, [SSD_D_INNER, SSD_D_INNER + SSD_BC_DIM], axis=-1)
    xs = xs.reshape(b, s, SSD_HEADS, SSD_HEAD_DIM)
    bm = bm.reshape(b, s, SSD_GROUPS, SSD_STATE)
    cm = cm.reshape(b, s, SSD_GROUPS, SSD_STATE)
    dt = jax.nn.softplus(dt_raw.astype(f32).reshape(b, s, 2, SSD_HEADS) + dt_bias.astype(f32))
    a = -jnp.exp(a_log.astype(f32))
    y_fwd = ssd_chunked(xs, dt[:, :, 0], a[0], bm, cm)
    def flip(t):
        return jnp.flip(t, axis=1)
    y_bwd = flip(ssd_chunked(flip(xs), flip(dt[:, :, 1]), a[1], flip(bm), flip(cm)))
    y = y_fwd + y_bwd + d_skip[:, None] * xs
    y = y.reshape(b, s, SSD_D_INNER) * jax.nn.silu(z)
    return rms_norm(y, norm_w)

def hierarchical_moe(h, w_rg, b_rg, w_re, b_re, w_gate, w_up, w_down):
    b, s, d = h.shape
    f32 = jnp.float32
    t = h.reshape(b * s, d)
    g_logits = (t @ w_rg + b_rg).astype(f32)
    g_sel = jnp.argmax(g_logits, axis=-1)
    g_gate = jnp.take_along_axis(jax.nn.softmax(g_logits, axis=-1), g_sel[:, None], axis=-1)
    e_logits = (t @ w_re + b_re).astype(f32).reshape(-1, N_EXPERT_GROUPS, EXPERTS_PER_GROUP)
    e_in = jnp.take_along_axis(e_logits, g_sel[:, None, None], axis=1)[:, 0]
    top_p, top_i = lax.top_k(jax.nn.softmax(e_in, axis=-1), EXPERT_TOP_K)
    combine = g_gate * top_p / jnp.sum(top_p, axis=-1, keepdims=True)
    expert_id = g_sel[:, None] * EXPERTS_PER_GROUP + top_i
    weights = jnp.sum(jax.nn.one_hot(expert_id, N_EXPERTS, dtype=f32) * combine[..., None], axis=1)
    weights = weights.astype(t.dtype)
    out = jnp.zeros_like(t)
    for gi in range(N_EXPERT_GROUPS):
        sl = slice(gi * EXPERTS_PER_GROUP, (gi + 1) * EXPERTS_PER_GROUP)
        hg = jnp.einsum('td,edf->tef', t, w_gate[sl])
        hu = jnp.einsum('td,edf->tef', t, w_up[sl])
        act = jax.nn.silu(hg) * hu * weights[:, sl, None]
        out = out + jnp.einsum('tef,efd->td', act, w_down[sl])
    return out.reshape(b, s, d)

def setup_inputs(seed: int = 0) -> dict:
    key = jax.random.key(seed)
    ks = jax.random.split(key, 24)
    f32 = jnp.float32
    def nrm(k, shape, scale):
        return jax.random.normal(k, shape, f32) * scale
    def gain(k, shape):
        return 1.0 + 0.02 * jax.random.normal(k, shape, f32)
    dt0 = jnp.exp(jax.random.uniform(ks[7], (DEPTH, 2, SSD_HEADS), f32, math.log(1e-3), math.log(1e-1)))
    return {
        'x': nrm(ks[0], (BATCH, SEQ, D_MODEL), 1.0),
        'attn_norm_w': gain(ks[1], (DEPTH, D_MODEL)),
        'w_in': nrm(ks[2], (DEPTH, D_MODEL, D_IN), D_MODEL ** -0.5),
        'swa_sink': nrm(ks[3], (DEPTH, SWA_HEADS), 0.5),
        'ssd_conv_w': nrm(ks[4], (DEPTH, SSD_CONV, SSD_CONV_DIM), SSD_CONV ** -0.5),
        'ssd_conv_b': nrm(ks[5], (DEPTH, SSD_CONV_DIM), 0.02),
        'ssd_dt_bias': dt0 + jnp.log(-jnp.expm1(-dt0)),
        'ssd_a_log': jnp.log(jax.random.uniform(ks[8], (DEPTH, 2, SSD_HEADS), f32, 1.0, 16.0)),
        'ssd_d': gain(ks[9], (DEPTH, SSD_HEADS)),
        'ssd_norm_w': gain(ks[10], (DEPTH, SSD_D_INNER)),
        'diff_lambda': nrm(ks[11], (DEPTH, 4, DIFF_QK_DIM), 0.1),
        'diff_subln_w': gain(ks[12], (DEPTH, DIFF_V_DIM)),
        'w_out': nrm(ks[13], (DEPTH, D_MIX, D_MODEL), D_MIX ** -0.5),
        'ffn_norm_w': gain(ks[14], (DEPTH, D_MODEL)),
        'w_router_group': nrm(ks[15], (DEPTH, D_MODEL, N_EXPERT_GROUPS), D_MODEL ** -0.5),
        'b_router_group': nrm(ks[16], (DEPTH, N_EXPERT_GROUPS), 0.01),
        'w_router_expert': nrm(ks[17], (DEPTH, D_MODEL, N_EXPERTS), D_MODEL ** -0.5),
        'b_router_expert': nrm(ks[18], (DEPTH, N_EXPERTS), 0.01),
        'w_gate': nrm(ks[19], (DEPTH, N_EXPERTS, D_MODEL, D_FF_EXPERT), D_MODEL ** -0.5),
        'w_up': nrm(ks[20], (DEPTH, N_EXPERTS, D_MODEL, D_FF_EXPERT), D_MODEL ** -0.5),
        'w_down': nrm(ks[21], (DEPTH, N_EXPERTS, D_FF_EXPERT, D_MODEL), D_FF_EXPERT ** -0.5),
        'final_norm_w': gain(ks[22], (D_MODEL,)),
    }

def reference(x, attn_norm_w, w_in, swa_sink, ssd_conv_w, ssd_conv_b, ssd_dt_bias, ssd_a_log, ssd_d,
              ssd_norm_w, diff_lambda, diff_subln_w, w_out, ffn_norm_w, w_router_group, b_router_group,
              w_router_expert, b_router_expert, w_gate, w_up, w_down, final_norm_w):
    b, s = x.shape[0], x.shape[1]
    slopes = alibi_slopes()
    swa_slopes, diff_slopes = slopes[:SWA_HEADS], slopes[SWA_HEADS:]
    sizes = [A_Q_DIM, A_KV_DIM, A_KV_DIM, SSD_D_INNER, SSD_CONV_DIM, SSD_DT_DIM,
             DIFF_QK_WIDTH, DIFF_QK_WIDTH, DIFF_V_WIDTH]
    offsets = [int(o) for o in np.cumsum(sizes)[:-1]]
    for l in range(DEPTH):
        h = rms_norm(x, attn_norm_w[l])
        proj = h @ w_in[l]
        a_q, a_k, a_v, b_z, b_xbc, b_dt, c_q, c_k, c_v = jnp.split(proj, offsets, axis=-1)
        y_a = windowed_gqa_sink(a_q.reshape(b, s, SWA_HEADS, HEAD_DIM),
                                a_k.reshape(b, s, SWA_KV_HEADS, HEAD_DIM),
                                a_v.reshape(b, s, SWA_KV_HEADS, HEAD_DIM), swa_sink[l], swa_slopes)
        y_b = ssd_mixer(b_z, b_xbc, b_dt, ssd_conv_w[l], ssd_conv_b[l], ssd_dt_bias[l], ssd_a_log[l],
                        ssd_d[l], ssd_norm_w[l])
        lambda_init = 0.8 - 0.6 * math.exp(-0.3 * l)
        y_c = diff_attention(c_q.reshape(b, s, DIFF_HEADS, 2, DIFF_QK_DIM),
                             c_k.reshape(b, s, DIFF_HEADS, 2, DIFF_QK_DIM),
                             c_v.reshape(b, s, DIFF_HEADS, DIFF_V_DIM),
                             diff_lambda[l], diff_subln_w[l], diff_slopes, lambda_init)
        x = x + jnp.concatenate([y_a, y_b, y_c], axis=-1) @ w_out[l]
        h = rms_norm(x, ffn_norm_w[l])
        x = x + hierarchical_moe(h, w_router_group[l], b_router_group[l], w_router_expert[l],
                                 b_router_expert[l], w_gate[l], w_up[l], w_down[l])
    return rms_norm(x, final_norm_w)


_drawn_inputs = setup_inputs


def setup_inputs(seed=0):
    import zlib

    import numpy as np

    out = dict(_drawn_inputs(seed))
    spreads = {}
    factors = {'swa_sink': 4.771,
     'diff_subln_w': 9.645,
     'b_router_group': 8.607,
     'b_router_expert': 9.336,
     'final_norm_w': 22.726,
     'ssd_d': 3.683,
     'ssd_norm_w': 2.834,
     'ffn_norm_w': 3.366}
    for name, (base, spread) in spreads.items():
        noise = np.random.default_rng([zlib.crc32(name.encode()), seed]).standard_normal(out[name].shape)
        drawn = base * np.exp(spread * noise) if base else spread * noise
        out[name] = __import__('jax').numpy.asarray(drawn.astype(out[name].dtype))
    for name, factor in factors.items():
        out[name] = (out[name] * factor).astype(out[name].dtype)
    return out
```

```python
import math
from contextlib import ExitStack

import concourse.bass as bass
from concourse import mybir

ALU = mybir.AluOpType
ACT = mybir.ActivationFunctionType
AX_X = mybir.AxisListType.X
F32 = mybir.dt.float32
BF16 = mybir.dt.bfloat16
I32 = mybir.dt.int32

P = 128
DEPTH, SEQ, D = 2, 256, 1024
TT = SEQ // P
KC = D // P
EPS = 1e-6
NEG = -1e30

A_H, A_KV, A_D = 6, 2, 64
REP = A_H // A_KV
WINDOW = 128
S_H, S_P, S_N, S_G, TAPS = 6, 64, 64, 2, 5
S_IN = S_H * S_P
S_REP = S_H // S_G
C_H, C_QK, C_V = 4, 32, 64
A_Q, A_K = A_H * A_D, A_KV * A_D
S_CONV = S_IN + 2 * S_G * S_N
CC = S_CONV // P
O_AQ = 0
O_AK = O_AQ + A_Q
O_AV = O_AK + A_K
O_Z = O_AV + A_K
O_XBC = O_Z + S_IN
O_DT = O_XBC + S_CONV
O_CQ = O_DT + 2 * S_H
O_CK = O_CQ + 2 * C_H * C_QK
O_CV = O_CK + 2 * C_H * C_QK
D_IN = O_CV + C_H * C_V
D_MIX = A_Q + S_IN + C_H * C_V
MC = D_MIX // P
SLOPE = [2.0 ** (-8.0 * (i + 1) / (A_H + C_H)) for i in range(A_H + C_H)]
A_SCALE, C_SCALE = A_D ** -0.5, C_QK ** -0.5

W_IN_PIECES = [(O_XBC, 512), (O_XBC + 512, O_CK - O_XBC - 512), (O_AQ, O_AV), (O_AV, O_XBC - O_AV), (O_CK, D_IN - O_CK)]
W_OUT_PIECES = [(0, 512), (512, 512)]
PIECES = len(W_IN_PIECES) + len(W_OUT_PIECES)
PW = 512

NG, EPG = 4, 8
NE = NG * EPG
FF = 512
FC = FF // P
SLOTS = 32
NQ = P // SLOTS
GQ, DQ = FF // NQ, D // NQ
EXTRA = 16
HALF = KC // 2
BATCHES = NE // NQ
TURNS = BATCHES // 2

K_AN, K_FN, K_CW, K_CB = 0, KC, 2 * KC, 2 * KC + CC * TAPS
NCOL = K_CB + CC
R_SN = 0
R_SL = R_SN + S_IN
R_D = R_SL + C_V
R_DTB = R_D + S_H
R_AL = R_DTB + 2 * S_H
R_SK = R_AL + 2 * S_H
R_LP = R_SK + A_H
R_LI = R_LP + 4 * C_QK
R_RB = R_LI + 2
NROW = R_RB + NG + NE


def mixer_steps():
    s = [("sq",), ("xn",)]
    s += [("xT", k) for k in range(KC)]
    s += [("par",), ("lam",)]
    s += [("xbc", c) for c in range(CC)] + [("dt",), ("conv", 0), ("conv", 1), ("dta",)]
    s += [("cq", 0), ("silu", 0), ("conv", 2), ("cq", 1), ("silu", 1), ("conv", 3)]
    s += [("aq", 0), ("silu", 2), ("conv", 4), ("aq", 1), ("silu", 3), ("aq", 2), ("silu", 4), ("ak",)]
    s += [("cum",), ("xs", 0), ("xs", 1), ("cb", 0), ("cb", 1), ("xdt",)]
    s += [("row", 0, 0), ("row", 0, 1), ("sc", 0), ("vz", 0), ("sc", 1), ("nm", 0), ("row", 1, 0), ("y", 0)]
    s += [("row", 1, 1), ("sc", 2), ("nm", 1), ("vz", 1), ("row", 2, 0), ("y", 1)]
    s += [("zs", 0), ("zs", 1), ("ck", 0), ("pT", 0), ("row", 2, 1), ("ck", 1), ("pT", 1)]
    s += [("sc", 3), ("nm", 2), ("row", 3, 0), ("y", 2), ("cv",), ("oa", 0), ("pT", 2)]
    s += [("sc", 4), ("nm", 3), ("row", 3, 1), ("pT", 3), ("oa", 1)]
    s += [("sc", 5), ("nm", 4), ("row", 4, 0), ("y", 3), ("pT", 4), ("sc", 6), ("nm", 5), ("row", 4, 1), ("pT", 5), ("oa", 2)]
    s += [("sc", 7), ("row", 5, 0), ("y", 4), ("sc", 8), ("nm", 6), ("row", 5, 1), ("pT", 6), ("sc", 9), ("y", 5), ("od", 0)]
    s += [("ybn",), ("sc", 10), ("nm", 7), ("pT", 7), ("sc", 11), ("od", 1), ("yT", 0), ("yT", 1)]
    s += [("sc", 12), ("nm", 8), ("pT", 8), ("sc", 13), ("od", 2), ("nm", 9), ("pT", 9), ("od", 3), ("ycn",), ("cT",)]
    s += [("out", t, h) for t in range(TT) for h in range(2)]
    s += [("sq2",), ("xn2",)] + [("fT", j) for j in range(KC // 2)]
    s += [("lg",), ("route",), ("acc",), ("rank",), ("ov1",), ("ov2",)]
    return s


STEPS = mixer_steps()
ON_PE = {"xT", "xbc", "dt", "cq", "aq", "ak", "cum", "xs", "cb", "row", "sc", "y", "vz", "pT", "ck", "cv", "oa", "od",
         "yT", "cT", "out", "acc", "fT", "lg", "rank", "ov1", "ov2"}
ON_DVE = {"sq", "xn", "par", "lam", "dt", "dta", "conv", "silu", "cum", "xdt", "row", "sc", "nm", "y", "zs", "ybn", "ycn", "out", "sq2",
          "lg", "route", "rank", "ov1", "ov2"}
ON_ACT = {"sq", "xn", "par", "lam", "dta", "silu", "row", "sc", "vz", "zs", "pT", "ck", "cv", "oa", "od", "yT", "cT", "cq",
          "aq", "ak", "xs", "cb", "sq2", "xn2", "route"}


def shared(step):
    return step[0] in ("xT", "xbc", "fT")


def on(engine, step):
    if engine == "pe":
        return step[0] in ON_PE
    if shared(step):
        return (step[1] % 2 == 0) == (engine == "act")
    return step[0] in (ON_DVE if engine == "dve" else ON_ACT)


COUNT = {e: {} for e in ("pe", "act", "dve")}
for _e in COUNT:
    for _s in STEPS:
        if on(_e, _s):
            COUNT[_e][_s] = len(COUNT[_e]) + 1

LAST_USE = [("xbc", 3), ("cq", 1), ("ak",), ("vz", 1), ("cv",)]

BANKS = 8
PE_STEPS = list(COUNT["pe"])
BANK = {}
for _s in PE_STEPS:
    BANK[_s] = len(BANK) % BANKS
BANK[("acc",)] = 0
for _j in range(KC // 2):
    BANK[("fT", _j)] = 4 + _j
for _j, _n in enumerate(("lg", "rank", "ov1", "ov2")):
    BANK[(_n,)] = 4 + _j


def reader(step):
    if shared(step):
        return "act" if step[1] % 2 == 0 else "dve"
    return "dve" if step[0] in ("dt", "cum", "sc", "y", "out", "lg", "rank", "ov1", "ov2") else "act"


def build_encoder(nc, x_in, cols, rows, w_in, w_out, w_router, w_gate, w_up, w_down, final_w, out):
    with ExitStack() as ctx:
        def sem(name):
            return ctx.enter_context(nc.semaphore(name))

        base = [-(-nc.sbuf_base // 64) * 64]

        def sb(name, shape, dt=F32, at=None):
            size = math.prod(shape[1:]) * (2 if dt == BF16 else 4)
            here = at[0] if at is not None else base[0]
            t = nc.alloc_sbuf_tensor_at(name, shape, dt, offset=here)
            (at if at is not None else base)[0] = here + -(-size // 64) * 64
            return t

        x = sb("x", [P, TT, D])
        ring = [sb(f"ring{i}", [P, KC * FF]) for i in range(6)]
        wm = [sb(f"wm{i}", [P, KC, PW]) for i in range(2)]
        wr = sb("wr", [P, KC, NG + NE])
        colp = sb("colp", [P, NCOL])
        rowp = sb("rowp", [P, NROW])
        ident = sb("ident", [P, P])
        identb = sb("identb", [P, P], BF16)
        upto = sb("upto", [P, P])
        since = sb("since", [P, P])
        before = sb("before", [P, P])
        ones = sb("ones", [P, P])
        smask = sb("smask", [P, 2, P], BF16)
        dist = sb("dist", [P, TT * P + P])
        distw = sb("distw", [P, TT * P + P])
        iota = sb("iota", [P, SEQ])
        tie = sb("tie", [P, NE])
        jcol = sb("jcol", [P, 2])
        prior = sb("prior", [1, 2])
        items = sb("items", [1, 2 * EXTRA + 2], I32)

        arena = base[0]
        m = [arena]
        xn = sb("xn", [P, TT, D], at=m)
        q = [arena]
        xdt = sb("xdt", [P, 2, TT, S_IN], at=q)
        pbuf2 = sb("pbuf2", [P, TT, SEQ], at=q)
        hT = sb("hT", [P, KC, SEQ], at=m)
        mixT = hT
        aqT = sb("aqT", [P, REP, SEQ], at=m)
        akT = sb("akT", [P, SEQ], at=m)
        cqT = sb("cqT", [P, 2, SEQ], at=m)
        ckT = sb("ckT", [P, 2, SEQ], at=m)
        q = [m[0]]
        PAD = SEQ + TAPS - 1
        xpad = sb("xpad", [P, CC, PAD], at=m)
        yb = sb("yb", [P, TT, S_IN], at=q)
        yc = sb("yc", [P, TT, C_H * C_V], at=q)
        q = [m[0]]
        xc = sb("xc", [P, CC, SEQ], at=m)
        E = [sb(f"E{i}", [P, 3, P], at=q) for i in range(2)]
        vz = sb("vz", [P, TT, PW], at=m)
        cv = sb("cv", [P, TT, C_H * C_V], at=m)
        pbuf = [sb("pbuf0", [P, TT, SEQ], at=m), sb("pbuf1", [P, TT, SEQ], at=m), pbuf2]
        ptb = [sb(f"ptb{i}", [P, TT, SEQ], at=m) for i in range(2)]
        xtok = sb("xtok", [P, TT, S_IN], at=m)
        CBs = sb("CBs", [P, S_G, TT, SEQ], at=m)
        tmp = sb("tmp", [P, S_IN], at=m)
        st = sb("st", [P, 32], at=m)
        dts = sb("dts", [P, TT, 2 * S_H], at=m)
        dta = sb("dta", [P, TT, 2 * S_H], at=m)
        sp = sb("sp", [P, 4, TT * 2 * S_H], at=m)
        cum = sb("cum", [P, TT, 3, 2 * S_H], at=m)
        den = sb("den", [P, 14, TT], at=m)
        nmx = sb("nmx", [P, 3, 14, TT], at=m)
        aneg = sb("aneg", [P, 2 * S_H], at=m)
        nsink = sb("nsink", [P, A_H], at=m)
        lam = sb("lam", [P, 4], at=m)
        lpt = sb("lpt", [P, 2, C_QK], at=m)
        slw = sb("slw", [P, C_V], at=m)
        m2 = [arena]
        xh = sb("xh", [P, TT, D], at=m2)
        hT2 = sb("hT2", [P, KC, SEQ], at=m2)
        st2 = sb("st2", [P, 8], at=m2)
        fnw = sb("fnw", [P, KC], at=m2)
        lgt = sb("lgt", [P, TT, NG + NE], at=m2)
        ga = sb("ga", [P, 4, TT, NG], at=m2)
        gs = sb("gs", [P, 12, TT], at=m2)
        em = sb("em", [P, 2, TT, NE], at=m2)
        ta = sb("ta", [P, TT, NE], at=m2)
        oh = sb("oh", [P, 2, TT, NE], at=m2)
        sel = sb("sel", [P, TT, NE], at=m2)
        R = sb("R", [P, TT, NE + NQ], at=m2)
        W = sb("W", [P, TT, NE + NQ], at=m2)
        cnt = sb("cnt", [NE, 12 + EXTRA], at=m2)
        ovd = sb("ovd", [EXTRA, 2, NE], at=m2)
        ovv = sb("ovv", [EXTRA, 2], at=m2)
        Pb = sb("Pb", [P, TT, P], at=m2)
        Pw = sb("Pw", [P, TT, P], at=m2)
        PwT = [sb(f"PwT{i}", [P, TT, P], at=m2) for i in range(2)]
        xg = [sb(f"xg{i}", [P, KC, P], at=m2) for i in range(2)]
        eg = sb("eg", [P, GQ], at=m2)
        sg = sb("sg", [P, GQ], at=m2)
        gu = sb("gu", [P, GQ], at=m2)
        actv = sb("actv", [P, GQ], at=m2)
        actT = sb("actT", [P, P], at=m2)
        ysb = sb("ysb", [P, D], at=m2)
        m3 = [m2[0]]
        fw = sb("fw", [P, D], at=m3)
        fin = sb("fin", [P, TT, D], at=m3)
        assert max(m[0], m2[0], m3[0]) <= nc.sbuf_usable_end, (m[0], m2[0], m3[0], nc.sbuf_usable_end)

        ps = [ctx.enter_context(nc.psum_tensor(f"ps{i}", [P, 512], F32)) for i in range(BANKS)]
        b_prep, b_gate, b_up, b_y = ps[4], ps[5], ps[6], ps[7]

        done = {e: sem(f"{e}_step_done") for e in ("pe", "act", "dve")}
        consts_ready, x_loaded, params_ready = sem("consts_ready"), sem("x_loaded"), sem("params_ready")
        piece_ready = [sem("piece_ready0"), sem("piece_ready1")]
        slot_ready = [sem(f"slot_ready{i}") for i in range(6)]
        waits_passed = sem("waits_passed")
        names = ("prep_ready", "prep_mm", "prep_copied", "gate_mm", "up_mm", "exp_ready", "act_ready", "actT_mm",
                 "actT_copied", "down_mm", "y_copied_act", "y_copied_dve", "combined")
        M = {n: sem(n) for n in names}
        V = {n: sem("extra_" + n) for n in names}
        extra_loaded = [sem(f"extra_loaded{i}") for i in range(3)]
        sums_read_dve, sums_read_act = sem("sums_read_dve"), sem("sums_read_act")
        final_act, final_dve, fw_loaded, stored = sem("final_act"), sem("final_dve"), sem("fw_loaded"), sem("stored")

        NCONST = 25

        from_one = [*done.values(), *M.values(), *V.values(), sums_read_dve, sums_read_act]

        def nth(li, who, step):
            return 1 + li * len(COUNT[who]) + COUNT[who][step]

        def piece_slot(n):
            return n % 2, (PIECES + 1 - n % 2) // 2

        def extras(eng):
            n = eng.value_load(items[0:1, 2 * EXTRA:2 * EXTRA + 1], min_val=0, max_val=EXTRA)
            before_n = eng.value_load(items[0:1, 2 * EXTRA + 1:2 * EXTRA + 2], min_val=0, max_val=DEPTH * EXTRA)
            return n, before_n

        def extra_item(eng, j):
            e = eng.value_load(items[0:1, bass.ds(j, 1)], min_val=0, max_val=NE - 1)
            r = eng.value_load(items[0:1, bass.ds(j + EXTRA, 1)], min_val=0, max_val=SEQ - SLOTS)
            return e, r

        block = ctx.enter_context(nc.Block())

        @block.sync
        def _(sp_):
            x_v = x_in.rearrange("o (t p) d -> p (o t) d", p=P)
            sp_.dma_start(x[:, :, :], x_v).then_inc(x_loaded, 16)
            gate_v = w_gate.rearrange("l e (p k) f -> (l e) p (k f)", k=KC)
            up_v = w_up.rearrange("l e (p k) f -> (l e) p (k f)", k=KC)
            down_v = w_down.rearrange("l e (c p) d -> (l e) p c d", p=P)

            def load_matrix(i, ge, at, signal):
                if i < 2:
                    src = (gate_v, up_v)[i][bass.ds(ge, 1), :, :].rearrange("o p n -> p (o n)")
                    sp_.dma_start(at[:, :], src).then_inc(signal, 16)
                else:
                    src = down_v[bass.ds(ge, 1), :, :, :].rearrange("o p c d -> p (o c) d")
                    sp_.dma_start(at[:, :].rearrange("p (c d) -> p c d", c=FC), src).then_inc(signal, 16)

            freed = (M["gate_mm"], M["up_mm"], M["down_mm"])

            def load_first(li, u, i):
                sp_.wait_ge(freed[i], 1 + li * NE)
                load_matrix(i, li * NE + u, ring[3 * u + i], slot_ready[3 * u + i])

            with sp_.Fori(0, DEPTH) as li:
                def load_piece(n):
                    if n >= 2:
                        sp_.wait_ge(done["pe"], nth(li, "pe", LAST_USE[n - 2]))
                        sp_.sem_inc(waits_passed, 1)
                    src, (c0, w) = ((w_in, W_IN_PIECES[n]) if n < len(W_IN_PIECES)
                                    else (w_out, W_OUT_PIECES[n - len(W_IN_PIECES)]))
                    s, _ = piece_slot(n)
                    v = src[bass.ds(li, 1), :, c0:c0 + w].rearrange("o (k p) n -> p (o k) n", p=P)
                    sp_.dma_start(wm[s][:, :, 0:w], v).then_inc(piece_ready[s], 16)

                sp_.wait_ge(done["pe"], 1 + li * len(COUNT["pe"]))
                sp_.sem_inc(waits_passed, 1)
                sp_.wait_ge(done["dve"], 1 + li * len(COUNT["dve"]))
                sp_.sem_inc(waits_passed, 1)
                load_piece(0)
                sp_.dma_start(colp[:, :], cols[bass.ds(li, 1), :, :].rearrange("o p n -> p (o n)")).then_inc(params_ready, 16)
                sp_.dma_start(rowp[:, :], rows[bass.ds(li, 1), :].rearrange("o n -> (o n)").partition_broadcast(P)
                              ).then_inc(params_ready, 16)
                sp_.dma_start(wr[:, :, :], w_router[bass.ds(li, 1), :, :].rearrange("o (p k) n -> p (o k) n", k=KC)
                              ).then_inc(params_ready, 16)

                load_piece(1)
                for n in range(2, PIECES):
                    load_first(li, (n - 2) // 3, (n - 2) % 3)
                    load_piece(n)
                load_first(li, 1, 2)
                with sp_.Fori(1, NE // 2) as p:
                    for u in range(2):
                        for i in range(3):
                            sp_.wait_ge(freed[i], 1 + li * NE + p * 2 + u - 1)
                            load_matrix(i, li * NE + p * 2 + u, ring[3 * u + i], slot_ready[3 * u + i])
                sp_.wait_ge(done["dve"], nth(li, "dve", ("ov2",)))
                sp_.sem_inc(waits_passed, 1)
                n, prev = extras(sp_)
                with sp_.If(n > 0):
                    sp_.wait_ge(M["combined"], 1 + (li + 1) * BATCHES)
                    sp_.sem_inc(waits_passed, 1)
                    with sp_.Fori(0, n) as j:
                        sp_.wait_ge(V["combined"], 1 + prev + j)
                        sp_.sem_inc(waits_passed, 1)
                        e, _ = extra_item(sp_, j)
                        for i in range(3):
                            load_matrix(i, li * NE + e, ring[i], extra_loaded[i])
                    sp_.wait_ge(V["combined"], 1 + prev + n)
                    sp_.sem_inc(waits_passed, 1)
            sp_.wait_ge(sums_read_dve, 1 + DEPTH)
            sp_.wait_ge(sums_read_act, 1 + DEPTH)
            sp_.dma_start(fw[:, :], final_w.partition_broadcast(P)).then_inc(fw_loaded, 16)
            out_v = out.rearrange("o (t p) d -> p (o t) d", p=P)
            for t in range(TT):
                sp_.wait_ge(final_dve, t + 2)
                sp_.dma_start(out_v[:, t, :], fin[:, t, :]).then_inc(stored, 16)
            sp_.wait_ge(stored, 16 * TT)


        @block.gpsimd
        def _(pool):
            g = nc.gpsimd
            n = [0]

            def put(ins):
                n[0] += 1
                ins.then_inc(consts_ready, 1)

            def sync():
                pool.wait_ge(consts_ready, n[0])

            for signal in from_one:
                pool.sem_inc(signal, 1)
            put(g.memset(ident[:, :], 0.0))
            for t in (upto, since, before, ones):
                put(g.memset(t[:, :], 1.0))
            put(g.memset(smask[:, :, :], 0.0))
            put(g.memset(prior[:, :], 0.0))
            put(g.iota(dist[:, :], pattern=[[-1, TT * P + P]], base=P, channel_multiplier=1,
                       allow_small_or_imprecise_dtypes=True))
            put(g.iota(iota[:, :], pattern=[[1, SEQ]], base=0, channel_multiplier=0,
                       allow_small_or_imprecise_dtypes=True))
            put(g.iota(tie[:, :], pattern=[[-1, NE]], base=64, channel_multiplier=0,
                       allow_small_or_imprecise_dtypes=True))
            put(g.iota(jcol[:, 0:1], pattern=[[0, 1]], base=0, channel_multiplier=1,
                       allow_small_or_imprecise_dtypes=True))
            put(g.iota(jcol[:, 1:2], pattern=[[0, 1]], base=SLOTS, channel_multiplier=SLOTS,
                       allow_small_or_imprecise_dtypes=True))
            sync()
            row = [[1, P]]
            back = [[-1, P]]
            put(g.affine_select(out=ident[:, :], in_=ident[:, :], compare_op=ALU.not_equal, fill=1.0, base=0,
                                pattern=back, channel_multiplier=1))
            put(g.affine_select(out=upto[:, :], in_=upto[:, :], compare_op=ALU.is_ge, fill=0.0, base=0,
                                pattern=row, channel_multiplier=-1))
            put(g.affine_select(out=since[:, :], in_=since[:, :], compare_op=ALU.is_ge, fill=0.0, base=0,
                                pattern=back, channel_multiplier=1))
            put(g.affine_select(out=before[:, :], in_=before[:, :], compare_op=ALU.is_ge, fill=0.0, base=-1,
                                pattern=row, channel_multiplier=-1))
            put(g.affine_select(out=smask[:, 0, :], in_=smask[:, 0, :], compare_op=ALU.is_ge, fill=NEG, base=0,
                                pattern=row, channel_multiplier=-1))
            put(g.affine_select(out=smask[:, 1, :], in_=smask[:, 1, :], compare_op=ALU.is_ge, fill=NEG, base=0,
                                pattern=back, channel_multiplier=1))
            put(g.tensor_scalar(distw[:, :], dist[:, :], -1.0, None, ALU.mult))
            sync()
            put(g.tensor_copy(identb[:, :], ident[:, :]))
            wide, ediw = [[-1, TT * P + P]], [[1, TT * P + P]]
            put(g.affine_select(out=distw[:, :], in_=distw[:, :], compare_op=ALU.is_ge, fill=0.0, base=P,
                                pattern=wide, channel_multiplier=1))
            put(g.affine_select(out=dist[:, :], in_=dist[:, :], compare_op=ALU.is_ge, fill=0.0, base=-P,
                                pattern=ediw, channel_multiplier=-1))
            sync()
            put(g.tensor_tensor(dist[:, :], dist[:, :], distw[:, :], ALU.add))
            sync()
            put(g.affine_select(out=distw[:, :], in_=dist[:, :], compare_op=ALU.is_ge, fill=NEG, base=P + WINDOW,
                                pattern=wide, channel_multiplier=1))
            sync()
            put(g.affine_select(out=distw[:, :], in_=distw[:, :], compare_op=ALU.is_ge, fill=NEG, base=WINDOW - P,
                                pattern=ediw, channel_multiplier=-1))
            assert n[0] == NCONST


        @block.tensor
        def _(pe):
            mm, tr = nc.tensor.matmul, nc.tensor.transpose
            pe.wait_ge(consts_ready, NCONST)

            def prep(S, b, n, part, w):
                if part == 0:
                    pe.wait_ge(S["prep_ready"], 1 + n)
                    for t in range(TT):
                        last = tr(b_prep[0:w, t * P:(t + 1) * P], Pw[:, t, 0:w], ident[:, :])
                else:
                    pe.wait_ge(S["prep_copied"], 3 * n - 2 + part)
                    for k in range(HALF):
                        for t in range(TT):
                            c = (part - 1) * HALF + k
                            last = mm(b_prep[:, k * w:(k + 1) * w], xh[:, t, c * P:(c + 1) * P], Pb[:, t, 0:w],
                                      start=(t == 0), stop=(t == TT - 1))
                last.then_inc(S["prep_mm"], 1)

            def hidden(S, b, u, bank, w, name):
                wv = w[:, :].rearrange("p (k f) -> p k f", k=KC)
                for k in range(KC):
                    for j in range(NQ):
                        last = mm(bank[j * SLOTS:(j + 1) * SLOTS, 0:GQ], xg[b][:, k, u * SLOTS:(u + 1) * SLOTS], wv[:, k, j * GQ:(j + 1) * GQ],
                                  start=(k == 0), stop=(k == KC - 1))
                last.then_inc(S[name], 1)

            def act_transpose(S, n):
                pe.wait_ge(S["act_ready"], 1 + n)
                tr(b_up[:, P:2 * P], actv[:, :], ident[:, :]).then_inc(S["actT_mm"], 1)

            def down(S, w, n):
                pe.wait_ge(S["y_copied_act"], n)
                pe.wait_ge(S["y_copied_dve"], n)
                wv = w[:, :].rearrange("p (c d) -> p c d", c=FC)
                for c in range(FC):
                    for j in range(NQ):
                        last = mm(b_y[j * SLOTS:(j + 1) * SLOTS, 0:DQ], actT[:, c * SLOTS:(c + 1) * SLOTS],
                                  wv[:, c, j * DQ:(j + 1) * DQ], start=(c == 0), stop=(c == FC - 1))
                last.then_inc(S["down_mm"], 1)

            def combine(S, b, n, w):
                for t in range(TT):
                    for h in range(2):
                        last = mm(ps[2 * t + h][:, :], PwT[b][0:w, t, :], ysb[0:w, h * PW:(h + 1) * PW],
                                  start=False, stop=False, skip_group_check=True)
                last.then_inc(S["combined"], 1)

            with pe.Fori(0, DEPTH) as li:
                def piece(n):
                    s, uses = piece_slot(n)
                    pe.wait_ge(piece_ready[s], (li * uses + n // 2 + 1) * 16)
                    return wm[s]

                for s in STEPS:
                    if not on("pe", s):
                        continue
                    kind = s[0]
                    bank = ps[BANK[s]]
                    i = PE_STEPS.index(s)
                    if i >= BANKS and kind not in ("acc", "fT", "lg", "rank", "ov1", "ov2"):
                        held = PE_STEPS[i - BANKS]
                        pe.wait_ge(done[reader(held)], nth(li, reader(held), held))
                    if kind == "xT":
                        if s[1] == 0:
                            pe.wait_ge(done["act"], nth(li, "act", ("xn",)))
                            pe.wait_ge(done["dve"], nth(li, "dve", ("xn",)))
                        for t in range(TT):
                            last = tr(bank[:, t * P:(t + 1) * P], xn[:, t, s[1] * P:(s[1] + 1) * P], ident[:, :])
                    elif kind in ("xbc", "cq", "aq", "ak", "ck"):
                        if s == ("xbc", 0):
                            w = piece(0)
                            pe.wait_ge(done["act"], nth(li, "act", ("xT", KC - 2)))
                            pe.wait_ge(done["dve"], nth(li, "dve", ("xT", KC - 1)))
                        elif s == ("xbc", 4):
                            w = piece(1)
                        elif s == ("aq", 0):
                            w = piece(2)
                        elif s == ("ck", 0):
                            w = piece(4)
                        c = s[1] if len(s) > 1 else 0
                        for k in range(KC):
                            if kind == "xbc":
                                lhs = w[:, k, (c % 4) * P:(c % 4 + 1) * P]
                            elif kind == "cq":
                                o = O_CQ - (O_XBC + 512) + c * P
                                lhs = w[:, k, o:o + P]
                            elif kind == "aq":
                                lhs = w[:, k, c * P:(c + 1) * P]
                            elif kind == "ak":
                                lhs = w[:, k, O_AK:O_AK + P]
                            else:
                                lhs = w[:, k, c * P:(c + 1) * P]
                            last = mm(bank[:, 0:SEQ], lhs, hT[:, k, :], start=(k == 0), stop=(k == KC - 1))
                    elif kind == "dt":
                        o = O_DT - (O_XBC + 512)
                        for t in range(TT):
                            for k in range(KC):
                                last = mm(bank[:, t * 2 * S_H:(t + 1) * 2 * S_H], hT[:, k, t * P:(t + 1) * P],
                                          w[:, k, o:o + 2 * S_H], start=(k == 0), stop=(k == KC - 1))
                    elif kind == "vz":
                        if s[1] == 0:
                            w = piece(3)
                        t = s[1]
                        for k in range(KC):
                            last = mm(bank[:, :], hT[:, k, t * P:(t + 1) * P], w[:, k, :], start=(k == 0), stop=(k == KC - 1))
                    elif kind == "cv":
                        for t in range(TT):
                            for k in range(KC):
                                last = mm(bank[:, t * C_H * C_V:(t + 1) * C_H * C_V], hT[:, k, t * P:(t + 1) * P],
                                          w[:, k, O_CV - O_CK:D_IN - O_CK], start=(k == 0), stop=(k == KC - 1))
                    elif kind == "cum":
                        pe.wait_ge(done["dve"], nth(li, "dve", ("dta",)))
                        for t in range(TT):
                            o = t * 4 * S_H
                            mm(bank[:, o:o + S_H], upto[:, :], dta[:, t, 0:S_H], start=True, stop=True)
                            mm(bank[:, o + S_H:o + 2 * S_H], since[:, :], dta[:, t, S_H:], start=True, stop=True)
                            last = mm(bank[:, o + 2 * S_H:o + 4 * S_H], ones[:, :], dta[:, t, :], start=True, stop=True)
                    elif kind == "xs":
                        pe.wait_ge(done["dve"], nth(li, "dve", ("silu", 2)))
                        t = s[1]
                        for c in range(S_IN // P):
                            last = tr(bank[:, c * P:(c + 1) * P], xc[:, c, t * P:(t + 1) * P], ident[:, :])
                    elif kind == "cb":
                        pe.wait_ge(done["dve"], nth(li, "dve", ("silu", 4)))
                        r = slice(s[1] * S_N, (s[1] + 1) * S_N)
                        for t in range(TT):
                            last = mm(bank[:, t * SEQ:(t + 1) * SEQ], xc[r, 3, t * P:(t + 1) * P], xc[r, 4, :],
                                      start=True, stop=True)
                    elif kind == "row":
                        _, h, d = s
                        tri = (upto, since)[d]
                        c = d * S_H + h
                        pe.wait_ge(done["dve"], nth(li, "dve", ("cum",)))
                        for o, t, masked in ((0, 0, True), (1, 1 - d, False), (2, 1, True)):
                            last = mm(bank[:, o * P:(o + 1) * P], dta[:, t, c:c + 1].broadcast_to([P, P]), tri[:, :],
                                      start=True, stop=not masked)
                            if masked:
                                last = mm(bank[:, o * P:(o + 1) * P], identb[:, :], smask[:, d, :], start=False, stop=True)
                    elif kind == "y":
                        h = s[1]
                        pe.wait_ge(done["dve"], nth(li, "dve", ("row", h, 1)))
                        pe.wait_ge(done["dve"], nth(li, "dve", ("xdt",)))
                        hs = slice(h * S_P, (h + 1) * S_P)
                        f, b = E[0], E[1]
                        for t, terms in ((0, ((f, 0, 0), (b, 0, 0), (b, 1, 1))), (1, ((f, 2, 1), (b, 2, 1), (f, 1, 0)))):
                            for n, (e, blk, src) in enumerate(terms):
                                last = mm(bank[:, t * S_P:(t + 1) * S_P], e[:, blk, :], xdt[:, 0 if e is f else 1, src, hs],
                                          start=(n == 0), stop=(n == 2))
                    elif kind == "sc":
                        u = s[1]
                        if u < A_H:
                            if u == 0:
                                pe.wait_ge(done["act"], nth(li, "act", ("ak",)))
                            r = slice((u // REP) * A_D, (u // REP + 1) * A_D)
                            ql, kr = aqT[r, u % REP, :], akT[r, :]
                        else:
                            h, mq = (u - A_H) // 2, (u - A_H) % 2
                            pe.wait_ge(done["act"], nth(li, "act", ("ck", h // 2)))
                            o = (2 * (h % 2) + mq) * C_QK
                            ql, kr = cqT[o:o + C_QK, h // 2, :], ckT[o:o + C_QK, h // 2, :]
                        for t in range(TT):
                            last = mm(bank[:, t * SEQ:(t + 1) * SEQ], ql[:, t * P:(t + 1) * P], kr, start=True, stop=True)
                    elif kind == "pT":
                        h = s[1]
                        pe.wait_ge(done["dve"], nth(li, "dve", ("nm", h)))
                        pb = pbuf[(h if h < A_H else A_H + 2 * (h - A_H)) % 3]
                        for kc in range(TT):
                            for t in range(TT):
                                last = tr(bank[:, kc * SEQ + t * P:kc * SEQ + (t + 1) * P], pb[:, t, kc * P:(kc + 1) * P],
                                          ident[:, :])
                    elif kind == "oa":
                        c = s[1]
                        pe.wait_ge(done["act"], nth(li, "act", ("pT", 2 * c + 1)))
                        for half in range(2):
                            h = 2 * c + half
                            for kc in range(TT):
                                g = h // REP
                                last = mm(bank[half * A_D:(half + 1) * A_D, 0:SEQ], vz[:, kc, g * A_D:(g + 1) * A_D],
                                          ptb[h % 2][:, kc, :], start=(kc == 0), stop=(kc == TT - 1))
                    elif kind == "od":
                        h = s[1]
                        pe.wait_ge(done["act"], nth(li, "act", ("pT", A_H + h)))
                        for t in range(TT):
                            for kc in range(TT):
                                last = mm(bank[:, t * C_V:(t + 1) * C_V], ptb[h % 2][:, kc, t * P:(t + 1) * P],
                                          cv[:, kc, h * C_V:(h + 1) * C_V], start=(kc == 0), stop=(kc == TT - 1))
                    elif kind == "yT":
                        pe.wait_ge(done["dve"], nth(li, "dve", ("ybn",)))
                        for c in range(S_IN // P):
                            last = tr(bank[:, c * P:(c + 1) * P], yb[:, s[1], c * P:(c + 1) * P], ident[:, :])
                    elif kind == "cT":
                        pe.wait_ge(done["dve"], nth(li, "dve", ("ycn",)))
                        for c in range(2):
                            for t in range(TT):
                                last = tr(bank[:, (c * TT + t) * P:(c * TT + t + 1) * P], yc[:, t, c * P:(c + 1) * P], ident[:, :])
                    elif kind == "out":
                        _, t, half = s
                        w = piece(5 + half)
                        pe.wait_ge(done["act"], nth(li, "act", ("cT",)))
                        for c in range(MC):
                            last = mm(bank[:, :], mixT[:, c, t * P:(t + 1) * P], w[:, c, :], start=(c == 0), stop=(c == MC - 1))
                    elif kind == "acc":
                        pe.wait_ge(done["dve"], nth(li, "dve", ("out", TT - 1, 1)))
                        for t in range(TT):
                            for h in range(2):
                                last = mm(ps[2 * t + h][:, :], ident[:, :], x[:, t, h * PW:(h + 1) * PW], start=True, stop=True)
                    elif kind == "fT":
                        if s[1] == 0:
                            pe.wait_ge(done["act"], nth(li, "act", ("xn2",)))
                        for a in range(2):
                            k = 2 * s[1] + a
                            for t in range(TT):
                                last = tr(bank[:, (a * TT + t) * P:(a * TT + t + 1) * P], xh[:, t, k * P:(k + 1) * P], ident[:, :])
                    elif kind == "lg":
                        pe.wait_ge(done["act"], nth(li, "act", ("fT", KC // 2 - 2)))
                        pe.wait_ge(done["dve"], nth(li, "dve", ("fT", KC // 2 - 1)))
                        pe.wait_ge(params_ready, (li + 1) * 48)
                        n = NG + NE
                        for t in range(TT):
                            for k in range(KC):
                                last = mm(bank[:, t * n:(t + 1) * n], hT2[:, k, t * P:(t + 1) * P], wr[:, k, :],
                                          start=(k == 0), stop=(k == KC - 1))
                    elif kind == "rank":
                        pe.wait_ge(done["dve"], nth(li, "dve", ("route",)))
                        mm(bank[:, 0:NE], before[:, :], sel[:, 0, :], start=True, stop=True)
                        mm(bank[:, NE:2 * NE], ones[:, :], sel[:, 0, :], start=True, stop=False)
                        mm(bank[:, NE:2 * NE], before[:, :], sel[:, 1, :], start=False, stop=True)
                        for t in range(TT):
                            last = mm(bank[0:NE, 2 * NE:2 * NE + 1], sel[:, t, :], ones[:, 0:1], start=(t == 0), stop=(t == 1))
                    elif kind == "ov1":
                        pe.wait_ge(done["dve"], nth(li, "dve", ("rank",)))
                        pe.sem_inc(waits_passed, 1)
                        mm(bank[0:EXTRA, 0:NE], cnt[:, 12:], upto[0:NE, 0:NE], start=True, stop=True)
                        last = mm(bank[0:EXTRA, NE:2 * NE], cnt[:, 12:], ident[0:NE, 0:NE], start=True, stop=True)
                    elif kind == "ov2":
                        pe.wait_ge(done["dve"], nth(li, "dve", ("ov1",)))
                        pe.sem_inc(waits_passed, 1)
                        for i in range(2):
                            mm(bank[0:1, i * EXTRA:(i + 1) * EXTRA], ovv[:, i:i + 1], ident[0:EXTRA, 0:EXTRA], start=True, stop=True)
                        last = mm(bank[0:1, 2 * EXTRA:2 * EXTRA + 1], cnt[:, 12:13], ones[0:NE, 0:1], start=True, stop=True)
                    last.then_inc(done["pe"], 1)

                g0 = li * (BATCHES + 1) + 1
                for part in range(3):
                    prep(M, 0, g0, part, P)
                with pe.Fori(0, TURNS) as turn:
                    for b in range(2):
                        g = g0 + turn * 2 + b
                        pe.wait_ge(M["prep_copied"], 1 + 3 * g)
                        for u in range(NQ):
                            r = 3 * (u % 2)
                            e = li * NE + (turn * 2 + b) * NQ + u + 1
                            used = li * (NE // 2) + turn * NQ + (b * NQ + u) // 2 + 1
                            pe.wait_ge(slot_ready[r], used * 16)
                            hidden(M, b, u, b_gate, ring[r], "gate_mm")
                            pe.wait_ge(slot_ready[r + 1], used * 16)
                            hidden(M, b, u, b_up, ring[r + 1], "up_mm")
                            if u < 3:
                                prep(M, 1 - b, g + 1, u, P)
                            act_transpose(M, e)
                            pe.wait_ge(slot_ready[r + 2], used * 16)
                            pe.wait_ge(M["actT_copied"], 1 + e)
                            down(M, ring[r + 2], e)
                        pe.wait_ge(M["y_copied_act"], 1 + e)
                        pe.wait_ge(M["y_copied_dve"], 1 + e)
                        combine(M, b, li * BATCHES + turn * 2 + b, P)
                pe.wait_ge(done["dve"], nth(li, "dve", ("ov2",)))
                pe.sem_inc(waits_passed, 1)
                n, prev = extras(pe)
                with pe.If(n > 0):
                    pe.wait_ge(M["prep_copied"], 1 + 3 * (li + 1) * (BATCHES + 1))
                    pe.sem_inc(waits_passed, 1)
                    with pe.Fori(0, n) as j:
                        e = prev + j + 1
                        for part in range(3):
                            prep(V, 0, e, part, SLOTS)
                        pe.wait_ge(V["prep_copied"], 1 + 3 * e)
                        pe.wait_ge(extra_loaded[0], e * 16)
                        hidden(V, 0, 0, b_gate, ring[0], "gate_mm")
                        pe.wait_ge(extra_loaded[1], e * 16)
                        hidden(V, 0, 0, b_up, ring[1], "up_mm")
                        act_transpose(V, e)
                        pe.wait_ge(extra_loaded[2], e * 16)
                        pe.wait_ge(V["actT_copied"], 1 + e)
                        down(V, ring[2], e)
                        pe.wait_ge(V["y_copied_act"], 1 + e)
                        pe.wait_ge(V["y_copied_dve"], 1 + e)
                        combine(V, 0, e, SLOTS)

        @block.scalar
        def _(act):
            A = nc.scalar.activation
            act.wait_ge(x_loaded, 16)
            act.wait_ge(consts_ready, NCONST)

            def act_exp(S, n):
                act.wait_ge(S["gate_mm"], 1 + n)
                A(eg[:, :], b_gate[:, 0:GQ], ACT.Exp, scale=-1.0).then_inc(S["exp_ready"], 1)

            def actT_copy(S, n):
                act.wait_ge(S["actT_mm"], 1 + n)
                A(actT[:, :], b_up[:, P:2 * P], ACT.Copy).then_inc(S["actT_copied"], 1)

            def y_copy(S, u, n):
                act.wait_ge(S["down_mm"], 1 + n)
                for j in range(NQ // 2):
                    last = A(ysb[u * SLOTS:(u + 1) * SLOTS, j * DQ:(j + 1) * DQ], b_y[j * SLOTS:(j + 1) * SLOTS, 0:DQ], ACT.Copy)
                last.then_inc(S["y_copied_act"], 1)

            with act.Fori(0, DEPTH) as li:
                act.wait_ge(sums_read_dve, 1 + li)
                act.sem_inc(waits_passed, 1)
                for s in STEPS:
                    if not on("act", s):
                        continue
                    kind = s[0]
                    bank = ps[BANK[s]] if s in BANK else None
                    act.drain()
                    if kind in ON_PE:
                        act.wait_ge(done["pe"], nth(li, "pe", s))
                    if kind == "sq":
                        last = A(xn[:, 1, :], x[:, 1, :], ACT.Square, accum_out=st[:, 1:2])
                    elif kind == "sq2":
                        act.wait_ge(done["dve"], nth(li, "dve", ("out", TT - 1, 1)))
                        last = A(xh[:, 1, :], x[:, 1, :], ACT.Square, accum_out=st2[:, 1:2])
                    elif kind == "xn":
                        act.wait_ge(done["dve"], nth(li, "dve", ("sq",)))
                        last = A(xn[:, 0, :], x[:, 0, :], ACT.Copy, scale=st[:, 2:3])
                    elif kind == "xn2":
                        act.wait_ge(done["dve"], nth(li, "dve", ("sq2",)))
                        A(fnw[:, :], colp[:, K_FN:K_FN + KC], ACT.Copy)
                        for t in range(TT):
                            last = A(xh[:, t, :].rearrange("p (k q) -> p k q", k=KC),
                                     x[:, t, :].rearrange("p (q k) -> p k q", k=KC), ACT.Copy, scale=st2[:, 2 + t:3 + t])
                    elif kind == "par":
                        act.wait_ge(params_ready, (li + 1) * 48)
                        last = A(aneg[:, :], rowp[:, R_AL:R_AL + 2 * S_H], ACT.Exp)
                    elif kind == "lam":
                        act.wait_ge(done["dve"], nth(li, "dve", ("par",)))
                        last = A(lam[:, 2:4], lam[:, 0:2], ACT.Exp)
                    elif kind == "dta":
                        act.wait_ge(done["dve"], nth(li, "dve", ("dt",)))
                        last = A(sp[:, 2, :], sp[:, 1, :], ACT.Exp)
                    elif kind == "xT":
                        if s[1] == 0:
                            act.wait_ge(params_ready, (li + 1) * 48)
                        last = A(hT[:, s[1], :], bank[:, 0:SEQ], ACT.Copy, scale=colp[:, K_AN + s[1]:K_AN + s[1] + 1])
                    elif kind == "xbc":
                        last = A(xpad[:, s[1], TAPS // 2:TAPS // 2 + SEQ], bank[:, 0:SEQ], ACT.Copy)
                    elif kind == "silu":
                        act.wait_ge(done["dve"], nth(li, "dve", ("conv", s[1])))
                        if s[1] > 0:
                            act.wait_ge(done["dve"], nth(li, "dve", ("silu", s[1] - 1)))
                        last = A(tmp[:, 0:SEQ], xc[:, s[1], :], ACT.Exp, scale=-1.0)
                    elif kind == "cq":
                        last = A(cqT[:, s[1], :], bank[:, 0:SEQ], ACT.Copy)
                    elif kind == "aq":
                        last = A(aqT[:, s[1], :], bank[:, 0:SEQ], ACT.Copy)
                    elif kind == "ak":
                        last = A(akT[:, :], bank[:, 0:SEQ], ACT.Copy)
                    elif kind == "ck":
                        last = A(ckT[:, s[1], :], bank[:, 0:SEQ], ACT.Copy)
                    elif kind == "cb":
                        last = A(CBs[:, s[1], :, :].rearrange("p a b -> p (a b)"), bank[:, :], ACT.Copy)
                    elif kind == "xs":
                        last = A(xtok[:, s[1], :], bank[:, 0:S_IN], ACT.Copy)
                    elif kind == "vz":
                        last = A(vz[:, s[1], :], bank[:, :], ACT.Copy)
                    elif kind == "cv":
                        last = A(cv[:, :, :].rearrange("p t n -> p (t n)"), bank[:, :], ACT.Copy)
                    elif kind == "zs":
                        act.wait_ge(done["dve"], nth(li, "dve", ("silu", 4))) if s[1] == 0 else act.wait_ge(done["dve"], nth(li, "dve", ("zs", 0)))
                        last = A(tmp[:, :], vz[:, s[1], A_K:], ACT.Exp, scale=-1.0)
                    elif kind == "row":
                        _, h, d = s
                        c = d * S_H + h
                        act.wait_ge(done["dve"], nth(li, "dve", ("cum",)))
                        if h == 0 and d == 0:
                            act.wait_ge(done["pe"], nth(li, "pe", ("xs", 1)))
                        if h > 0:
                            act.wait_ge(done["pe"], nth(li, "pe", ("y", h - 1)))
                        A(E[d][:, 0, :], bank[:, 0:P], ACT.Exp, bias=cum[:, 0, 0, c:c + 1])
                        A(E[d][:, 1, :], bank[:, P:2 * P], ACT.Exp, bias=cum[:, d, 2, c:c + 1])
                        last = A(E[d][:, 2, :], bank[:, 2 * P:3 * P], ACT.Exp, bias=cum[:, 1, 0, c:c + 1])
                    elif kind == "sc":
                        u = s[1]
                        act.wait_ge(done["dve"], nth(li, "dve", ("sc", u)))
                        pb = pbuf[u % 3]
                        for t in range(TT):
                            last = A(pb[:, t, :], pb[:, t, :], ACT.Exp, bias=nmx[:, 1, u, t:t + 1],
                                     scale=A_SCALE if u < A_H else C_SCALE, accum_out=den[:, u, t:t + 1])
                        if u < A_H:
                            last = A(nmx[:, 2, u, :], nmx[:, 1, u, :], ACT.Exp, bias=rowp[:, R_SK + u:R_SK + u + 1])
                    elif kind == "pT":
                        h = s[1]
                        if h >= 2:
                            if h < A_H:
                                act.wait_ge(done["pe"], nth(li, "pe", ("oa", h // 2 - 1)))
                            elif h < A_H + 2:
                                act.wait_ge(done["pe"], nth(li, "pe", ("oa", 2)))
                            else:
                                act.wait_ge(done["pe"], nth(li, "pe", ("od", h - A_H - 2)))
                        last = A(ptb[h % 2][:, :, :].rearrange("p a b -> p (a b)"), bank[:, :], ACT.Copy)
                    elif kind == "oa":
                        act.wait_ge(done["pe"], nth(li, "pe", ("cv",)))
                        last = A(mixT[:, s[1], :], bank[:, 0:SEQ], ACT.Copy)
                    elif kind == "od":
                        last = A(yc[:, :, s[1] * C_V:(s[1] + 1) * C_V],
                                 bank[:, 0:TT * C_V].rearrange("p (t v) -> p t v", t=TT), ACT.Copy)
                    elif kind == "yT":
                        last = A(mixT[:, REP:2 * REP, s[1] * P:(s[1] + 1) * P],
                                 bank[:, 0:S_IN].rearrange("p (c t) -> p c t", c=S_IN // P), ACT.Copy)
                    elif kind == "cT":
                        last = A(mixT[:, 2 * REP:MC, :].rearrange("p c t -> p (c t)"), bank[:, :], ACT.Copy)
                    elif kind == "fT":
                        for a in range(2):
                            k = 2 * s[1] + a
                            last = A(hT2[:, k, :], bank[:, a * SEQ:(a + 1) * SEQ], ACT.Copy, scale=colp[:, K_FN + k:K_FN + k + 1])
                    elif kind == "route":
                        act.wait_ge(done["dve"], nth(li, "dve", ("lg",)))
                        A(ga[:, 3, :, :], ga[:, 0, :, :], ACT.Exp)
                        last = A(gs[:, 5, :], gs[:, 4, :], ACT.Exp)
                    last.then_inc(done["act"], 1)

                with act.Fori(0, BATCHES) as g:
                    for u in range(NQ):
                        e = li * NE + g * NQ + u + 1
                        act_exp(M, e)
                        actT_copy(M, e)
                        y_copy(M, u, e)
                act.wait_ge(done["dve"], nth(li, "dve", ("ov2",)))
                act.sem_inc(waits_passed, 1)
                n, prev = extras(act)
                with act.If(n > 0):
                    with act.Fori(0, n) as j:
                        e = prev + j + 1
                        act_exp(V, e)
                        actT_copy(V, e)
                        y_copy(V, 0, e)
                act.wait_ge(M["combined"], 1 + (li + 1) * BATCHES)
                act.wait_ge(V["combined"], 1 + prev + n)
                for h in range(2):
                    last = A(x[:, 1, h * PW:(h + 1) * PW], ps[2 + h][:, :], ACT.Copy)
                last.then_inc(sums_read_act, 1)
            act.drain()
            act.wait_ge(sums_read_dve, 1 + DEPTH)
            A(xh[:, 1, :], x[:, 1, :], ACT.Square, accum_out=st2[:, 1:2]).then_inc(final_act, 1)

        @block.vector
        def _(dve):
            v = nc.vector
            dve.wait_ge(consts_ready, NCONST)
            dve.wait_ge(x_loaded, 16)

            def rsqrt(s, n, scale):
                val, y, a, b = (s[:, i * n:(i + 1) * n] for i in range(4))
                dve.drain()
                v.tensor_scalar(val, val, scale, EPS, ALU.mult, ALU.add)
                dve.drain()
                v.tensor_scalar(a.bitcast(I32), val.bitcast(I32), 1, None, ALU.logical_shift_right)
                dve.drain()
                v.tensor_scalar(y.bitcast(I32), a.bitcast(I32), -1.0, 1597463007.0, ALU.mult, ALU.add)
                for _ in range(3):
                    dve.drain()
                    v.tensor_tensor(a, y, y, ALU.mult)
                    dve.drain()
                    v.scalar_tensor_tensor(b, a, -0.5, val, ALU.mult, ALU.mult)
                    dve.drain()
                    last = v.scalar_tensor_tensor(y, b, 1.5, y, ALU.add, ALU.mult)
                return last

            def prep(g):
                four = [P, TT, NQ, SLOTS]
                one_hot, weighted = (p[:, :, :].rearrange("p t (e s) -> p t e s", e=NQ) for p in (Pb, Pw))
                v.tensor_tensor(one_hot, iota[:, 0:SLOTS].unsqueeze(1).unsqueeze(1).broadcast_to(four),
                                R[:, :, bass.ds(g * NQ, NQ)].unsqueeze(3).broadcast_to(four), ALU.is_equal)
                dve.drain()
                v.tensor_tensor(weighted, one_hot, W[:, :, bass.ds(g * NQ, NQ)].unsqueeze(3).broadcast_to(four), ALU.mult
                                ).then_inc(M["prep_ready"], 1)

            def prep_extra(e, r0):
                for t in range(TT):
                    rank = R[:, t, bass.ds(e, 1)]
                    v.tensor_scalar(Pb[:, t, 0:SLOTS], iota[:, bass.ds(r0, SLOTS)], rank, None, ALU.is_equal)
                    last = v.tensor_scalar(Pw[:, t, 0:SLOTS], iota[:, bass.ds(r0, SLOTS)], rank, W[:, t, bass.ds(e, 1)],
                                           ALU.is_equal, ALU.mult)
                last.then_inc(V["prep_ready"], 1)

            def activate(S, n):
                dve.drain()
                dve.wait_ge(S["exp_ready"], 1 + n)
                v.tensor_scalar(sg[:, :], eg[:, :], 1.0, None, ALU.add)
                dve.drain()
                v.reciprocal(eg[:, :], sg[:, :])
                dve.drain()
                v.tensor_tensor(gu[:, :], eg[:, :], b_gate[:, 0:GQ], ALU.mult)
                dve.drain()
                dve.wait_ge(S["up_mm"], 1 + n)
                v.tensor_tensor(actv[:, :], gu[:, :], b_up[:, 0:GQ], ALU.mult).then_inc(S["act_ready"], 1)

            def prep_copy(S, b, n, part, w):
                dve.wait_ge(S["prep_mm"], 3 * n - 1 + part)
                if part == 0:
                    last = v.tensor_copy(PwT[b][0:w, :, :].rearrange("p t c -> p (t c)"), b_prep[0:w, 0:SEQ])
                else:
                    ks = slice((part - 1) * HALF, part * HALF)
                    last = v.tensor_tensor(xg[b][:, ks, 0:w], b_prep[:, 0:HALF * w].rearrange("p (k c) -> p k c", k=HALF),
                                           fnw[:, ks].unsqueeze(2).broadcast_to([P, HALF, w]), ALU.mult)
                last.then_inc(S["prep_copied"], 1)

            def y_copy(S, u, n):
                dve.wait_ge(S["down_mm"], 1 + n)
                for j in range(NQ // 2, NQ):
                    last = v.tensor_copy(ysb[u * SLOTS:(u + 1) * SLOTS, j * DQ:(j + 1) * DQ], b_y[j * SLOTS:(j + 1) * SLOTS, 0:DQ])
                last.then_inc(S["y_copied_dve"], 1)

            with dve.Fori(0, DEPTH) as li:
                dve.wait_ge(sums_read_act, 1 + li)
                dve.sem_inc(waits_passed, 1)
                for s in STEPS:
                    if not on("dve", s):
                        continue
                    kind = s[0]
                    bank = ps[BANK[s]] if s in BANK else None
                    dve.drain()
                    if kind in ON_PE:
                        dve.wait_ge(done["pe"], nth(li, "pe", s))
                    if kind in ("sq", "sq2"):
                        xx, buf = (xn, st) if kind == "sq" else (xh, st2)
                        v.scalar_tensor_tensor(xx[:, 0, :], x[:, 0, :], 1.0, x[:, 0, :], ALU.mult, ALU.mult,
                                               accum_out=buf[:, 0:1])
                        dve.wait_ge(done["act"], nth(li, "act", (kind,)))
                        dve.sem_inc(waits_passed, 1)
                        last = rsqrt(buf, TT, 1.0 / D)
                    elif kind == "xn":
                        last = v.tensor_scalar(xn[:, 1, :], x[:, 1, :], st[:, 3:4], None, ALU.mult)
                    elif kind == "xT":
                        if s[1] == 1:
                            dve.wait_ge(params_ready, (li + 1) * 48)
                        last = v.tensor_scalar(hT[:, s[1], :], bank[:, 0:SEQ], colp[:, K_AN + s[1]:K_AN + s[1] + 1], None, ALU.mult)
                    elif kind == "par":
                        dve.wait_ge(done["act"], nth(li, "act", ("par",)))
                        v.tensor_scalar(nsink[:, :], rowp[:, R_SK:R_SK + A_H], -1.0, None, ALU.mult)
                        v.memset(xpad[:, :, 0:TAPS // 2], 0.0)
                        v.memset(xpad[:, :, TAPS // 2 + SEQ:], 0.0)
                        v.tensor_scalar(slw[:, :], rowp[:, R_SL:R_SL + C_V], rowp[:, R_LI + 1:R_LI + 2], None, ALU.mult)
                        lp = rowp[:, R_LP:R_LP + 4 * C_QK].rearrange("p (a b d) -> p a b d", a=2, b=2)
                        v.tensor_tensor(lpt[:, :, :], lp[:, :, 0, :], lp[:, :, 1, :], ALU.mult)
                        dve.drain()
                        v.tensor_scalar(aneg[:, :], aneg[:, :], -1.0, None, ALU.mult)
                        dve.drain()
                        last = v.tensor_reduce(lam[:, 0:2], lpt[:, :, :], AX_X, ALU.add)
                    elif kind == "xbc":
                        last = v.tensor_copy(xpad[:, s[1], TAPS // 2:TAPS // 2 + SEQ], bank[:, 0:SEQ])
                    elif kind == "dt":
                        n = 2 * S_H
                        z, a, b, c = (sp[:, i, :] for i in range(4))
                        v.tensor_tensor(sp[:, 0, :].rearrange("p (t n) -> p t n", t=TT),
                                        bank[:, 0:TT * n].rearrange("p (t n) -> p t n", t=TT),
                                        rowp[:, R_DTB:R_DTB + n].unsqueeze(1).broadcast_to([P, TT, n]), ALU.add)
                        dve.drain()
                        last = v.scalar_tensor_tensor(a, z, -1.0, z, ALU.mult, ALU.min)
                    elif kind == "conv":
                        c = s[1]
                        dve.wait_ge(done["act" if c % 2 == 0 else "dve"], nth(li, "act" if c % 2 == 0 else "dve", ("xbc", c)))
                        k = K_CW + c * TAPS
                        v.tensor_scalar(xc[:, c, :], xpad[:, c, 0:SEQ], colp[:, k:k + 1],
                             colp[:, K_CB + c:K_CB + c + 1], ALU.mult, ALU.add)
                        for j in range(1, TAPS):
                            dve.drain()
                            last = v.scalar_tensor_tensor(xc[:, c, :], xpad[:, c, j:j + SEQ],
                                                          colp[:, k + j:k + j + 1], xc[:, c, :], ALU.mult, ALU.add)
                    elif kind == "silu":
                        dve.wait_ge(done["act"], nth(li, "act", s))
                        c = s[1]
                        v.tensor_scalar(tmp[:, 0:SEQ], tmp[:, 0:SEQ], 1.0, None, ALU.add)
                        dve.drain()
                        v.reciprocal(tmp[:, 0:SEQ], tmp[:, 0:SEQ])
                        dve.drain()
                        last = v.tensor_tensor(xc[:, c, :], xc[:, c, :], tmp[:, 0:SEQ], ALU.mult)
                    elif kind == "zs":
                        dve.wait_ge(done["act"], nth(li, "act", s))
                        t = s[1]
                        v.tensor_scalar(tmp[:, :], tmp[:, :], 1.0, None, ALU.add)
                        dve.drain()
                        v.reciprocal(tmp[:, :], tmp[:, :])
                        dve.drain()
                        last = v.tensor_tensor(vz[:, t, A_K:], vz[:, t, A_K:], tmp[:, :], ALU.mult)
                    elif kind == "lam":
                        dve.wait_ge(done["act"], nth(li, "act", ("lam",)))
                        last = v.tensor_scalar(lam[:, 0:1], lam[:, 3:4], lam[:, 2:3], rowp[:, R_LI:R_LI + 1],
                                    ALU.subtract, ALU.subtract)
                    elif kind == "dta":
                        dve.wait_ge(done["act"], nth(li, "act", ("dta",)))
                        n = 2 * S_H
                        z, a, u, c = (sp[:, i, :] for i in range(4))
                        v.tensor_scalar(a, u, 2.0, None, ALU.add)
                        dve.drain()
                        v.reciprocal(a, a)
                        dve.drain()
                        v.tensor_tensor(u, u, a, ALU.mult)
                        dve.drain()
                        v.tensor_tensor(a, u, u, ALU.mult)
                        dve.drain()
                        v.tensor_scalar(c, a, 1.0 / 17, None, ALU.mult)
                        for j in (15, 13, 11, 9, 7, 5, 3):
                            dve.drain()
                            v.scalar_tensor_tensor(c, c, 1.0 / j, a, ALU.add, ALU.mult)
                        dve.drain()
                        v.scalar_tensor_tensor(c, c, 1.0, u, ALU.add, ALU.mult)
                        dve.drain()
                        v.tensor_scalar(z, z, 0.0, None, ALU.max)
                        dve.drain()
                        v.scalar_tensor_tensor(dts[:, :, :].rearrange("p t n -> p (t n)"), c, 2.0, z, ALU.mult, ALU.add)
                        dve.drain()
                        last = v.tensor_tensor(dta[:, :, :], dts[:, :, :],
                                               aneg[:, :].unsqueeze(1).broadcast_to([P, TT, n]), ALU.mult)
                    elif kind == "cum":
                        n = 2 * S_H
                        src = bank[:, 0:TT * 2 * n].rearrange("p (t k n) -> p t k n", t=TT, k=2)
                        v.tensor_scalar(cum[:, :, 0, :], src[:, :, 0, :], -1.0, None, ALU.mult)
                        v.tensor_copy(cum[:, :, 1, :], src[:, :, 1, :])
                        dve.drain()
                        last = v.tensor_tensor(cum[:, :, 2, :], cum[:, :, 1, :], cum[:, :, 0, :], ALU.add)
                    elif kind == "xdt":
                        dve.wait_ge(done["act"], nth(li, "act", ("xs", 1)))
                        for d in range(2):
                            for t in range(TT):
                                last = v.tensor_tensor(
                                    xdt[:, d, t, :].rearrange("p (h i) -> p h i", h=S_H),
                                    xtok[:, t, :].rearrange("p (h i) -> p h i", h=S_H),
                                    dts[:, t, d * S_H:(d + 1) * S_H].unsqueeze(2).broadcast_to([P, S_H, S_P]), ALU.mult)
                    elif kind == "row":
                        dve.wait_ge(done["act"], nth(li, "act", s))
                        _, h, d = s
                        g = h // S_REP
                        if h == 0 and d == 0:
                            dve.wait_ge(done["act"], nth(li, "act", ("cb", 1)))
                        e, cb = E[d], CBs[:, g, :, :]
                        ef = e[:, :, :].rearrange("p b t -> p (b t)")
                        if d == 0:
                            v.tensor_tensor(ef[:, 0:SEQ], ef[:, 0:SEQ], cb[:, 0, :], ALU.mult)
                            last = v.tensor_tensor(ef[:, SEQ:], ef[:, SEQ:], cb[:, 1, P:], ALU.mult)
                        else:
                            v.tensor_tensor(ef[:, 0:P], ef[:, 0:P], cb[:, 0, 0:P], ALU.mult)
                            last = v.tensor_tensor(ef[:, P:], ef[:, P:], cb[:, 1, :], ALU.mult)
                    elif kind == "y":
                        h = s[1]
                        hs = slice(h * S_P, (h + 1) * S_P)
                        last = v.scalar_tensor_tensor(yb[:, :, hs], xtok[:, :, hs], rowp[:, R_D + h:R_D + h + 1],
                                                      bank[:, 0:TT * S_P].rearrange("p (t i) -> p t i", t=TT), ALU.mult, ALU.add)
                    elif kind == "sc":
                        u = s[1]
                        if u >= 3:
                            w = u - 3
                            if w < A_H:
                                dve.wait_ge(done["pe"], nth(li, "pe", ("pT", w)))
                            elif (w - A_H) % 2 == 0:
                                dve.wait_ge(done["pe"], nth(li, "pe", ("pT", A_H + (w - A_H) // 2)))
                        pb = pbuf[u % 3]
                        table, slope = ((distw, SLOPE[u] / A_SCALE) if u < A_H
                                        else (dist, SLOPE[A_H + (u - A_H) // 2] / C_SCALE))
                        for t in range(TT):
                            o = P * (1 - t)
                            v.scalar_tensor_tensor(pb[:, t, :], table[:, o:o + SEQ], slope, bank[:, t * SEQ:(t + 1) * SEQ],
                                                   ALU.mult, ALU.add)
                        dve.drain()
                        v.reduce_max(nmx[:, 0, u, :], pb[:, :, :], AX_X)
                        if u < A_H:
                            dve.drain()
                            last = v.tensor_scalar(nmx[:, 1, u, :], nmx[:, 0, u, :], -A_SCALE, nsink[:, u:u + 1],
                                                   ALU.mult, ALU.min)
                        else:
                            dve.drain()
                            last = v.tensor_scalar(nmx[:, 1, u, :], nmx[:, 0, u, :], -C_SCALE, None, ALU.mult)
                    elif kind == "nm":
                        h = s[1]
                        if h < A_H:
                            u = h
                            dve.wait_ge(done["act"], nth(li, "act", ("sc", u)))
                            v.tensor_tensor(den[:, u, :], den[:, u, :], nmx[:, 2, u, :], ALU.add)
                            dve.drain()
                            v.reciprocal(den[:, u, :], den[:, u, :])
                            dve.drain()
                            for t in range(TT):
                                last = v.tensor_scalar(pbuf[u % 3][:, t, :], pbuf[u % 3][:, t, :], den[:, u, t:t + 1], None, ALU.mult)
                        else:
                            u = A_H + 2 * (h - A_H)
                            dve.wait_ge(done["act"], nth(li, "act", ("sc", u + 1)))
                            p0, p1 = pbuf[u % 3], pbuf[(u + 1) % 3]
                            v.reciprocal(den[:, u:u + 2, :], den[:, u:u + 2, :])
                            dve.drain()
                            v.tensor_scalar(den[:, u + 1, :], den[:, u + 1, :], lam[:, 0:1], None, ALU.mult)
                            for t in range(TT):
                                v.tensor_scalar(p0[:, t, :], p0[:, t, :], den[:, u, t:t + 1], None, ALU.mult)
                            dve.drain()
                            for t in range(TT):
                                last = v.scalar_tensor_tensor(p0[:, t, :], p1[:, t, :], den[:, u + 1, t:t + 1], p0[:, t, :],
                                                              ALU.mult, ALU.add)
                    elif kind == "ybn":
                        v.tensor_tensor(yb[:, :, :], yb[:, :, :], vz[:, :, A_K:], ALU.mult)
                        for t in range(TT):
                            dve.drain()
                            v.scalar_tensor_tensor(tmp[:, :], yb[:, t, :], 1.0, yb[:, t, :], ALU.mult, ALU.mult,
                                                   accum_out=st[:, t:t + 1])
                        rsqrt(st, TT, 1.0 / S_IN)
                        dve.drain()
                        for t in range(TT):
                            last = v.scalar_tensor_tensor(yb[:, t, :], yb[:, t, :], st[:, TT + t:TT + t + 1],
                                                          rowp[:, R_SN:R_SN + S_IN], ALU.mult, ALU.mult)
                    elif kind == "ycn":
                        dve.wait_ge(done["act"], nth(li, "act", ("od", C_H - 1)))
                        n = TT * C_H
                        ycf = yc[:, :, :].rearrange("p t (h i) -> p (t h) i", h=C_H)
                        sqf = xtok[:, :, :].rearrange("p t n -> p (t n)")[:, 0:n * C_V].rearrange("p (g i) -> p g i", g=n)
                        v.tensor_tensor(sqf, ycf, ycf, ALU.mult)
                        dve.drain()
                        v.tensor_reduce(st[:, 0:n], sqf, AX_X, ALU.add)
                        rsqrt(st, n, 1.0 / C_V)
                        dve.drain()
                        v.tensor_tensor(ycf, ycf, st[:, n:2 * n].unsqueeze(2).broadcast_to([P, n, C_V]), ALU.mult)
                        dve.drain()
                        last = v.tensor_tensor(ycf, ycf, slw[:, :].unsqueeze(1).broadcast_to([P, n, C_V]), ALU.mult)
                    elif kind == "out":
                        _, t, half = s
                        hs = slice(half * PW, (half + 1) * PW)
                        last = v.tensor_tensor(x[:, t, hs], x[:, t, hs], bank[:, :], ALU.add)
                    elif kind == "fT":
                        for a in range(2):
                            k = 2 * s[1] + a
                            last = v.tensor_scalar(hT2[:, k, :], bank[:, a * SEQ:(a + 1) * SEQ],
                                                   colp[:, K_FN + k:K_FN + k + 1], None, ALU.mult)
                    elif kind == "lg":
                        n = NG + NE
                        v.memset(R[:, :, NE:], -1.0)
                        v.memset(W[:, :, NE:], 0.0)
                        v.tensor_tensor(lgt[:, :, :], bank[:, 0:TT * n].rearrange("p (t n) -> p t n", t=TT),
                                        rowp[:, R_RB:R_RB + n].unsqueeze(1).broadcast_to([P, TT, n]), ALU.add)
                        L, Eq = lgt[:, :, 0:NG], lgt[:, :, NG:]

                        def first_of(one_hot, vals, top, score, key, k):
                            dve.drain()
                            v.tensor_tensor(score, vals, top.unsqueeze(2).broadcast_to([P, TT, k]), ALU.is_equal)
                            dve.drain()
                            v.tensor_tensor(score, score, tie[:, 0:k].unsqueeze(1).broadcast_to([P, TT, k]), ALU.mult)
                            dve.drain()
                            v.reduce_max(key, score, AX_X)
                            dve.drain()
                            return v.tensor_tensor(one_hot, score, key.unsqueeze(2).broadcast_to([P, TT, k]), ALU.is_equal)

                        dve.drain()
                        v.reduce_max(gs[:, 0, :], L, AX_X)
                        dve.drain()
                        v.tensor_tensor(ga[:, 0, :, :], L, gs[:, 0, :].unsqueeze(2).broadcast_to([P, TT, NG]), ALU.subtract)
                        first_of(ga[:, 2, :, :], L, gs[:, 0, :], ga[:, 1, :, :], gs[:, 1, :], NG)
                        dve.drain()
                        v.tensor_scalar(ga[:, 1, :, :], ga[:, 2, :, :], -1.0, -NEG, ALU.add, ALU.mult)
                        dve.drain()
                        v.tensor_tensor(em[:, 0, :, :].rearrange("p t (g e) -> p t g e", g=NG),
                                        Eq.rearrange("p t (g e) -> p t g e", g=NG),
                                        ga[:, 1, :, :].unsqueeze(3).broadcast_to([P, TT, NG, EPG]), ALU.add)
                        dve.drain()
                        v.reduce_max(gs[:, 2, :], em[:, 0, :, :], AX_X)
                        first_of(oh[:, 0, :, :], em[:, 0, :, :], gs[:, 2, :], ta[:, :, :], gs[:, 1, :], NE)
                        dve.drain()
                        v.scalar_tensor_tensor(em[:, 1, :, :], oh[:, 0, :, :], 3 * NEG, em[:, 0, :, :], ALU.mult, ALU.add)
                        dve.drain()
                        v.reduce_max(gs[:, 3, :], em[:, 1, :, :], AX_X)
                        dve.drain()
                        v.tensor_tensor(gs[:, 4, :], gs[:, 3, :], gs[:, 2, :], ALU.subtract)
                        last = first_of(oh[:, 1, :, :], em[:, 1, :, :], gs[:, 3, :], ta[:, :, :], gs[:, 1, :], NE)
                    elif kind == "route":
                        dve.wait_ge(done["act"], nth(li, "act", ("route",)))
                        v.tensor_reduce(gs[:, 6, :], ga[:, 3, :, :], AX_X, ALU.add)
                        dve.drain()
                        v.scalar_tensor_tensor(gs[:, 7, :], gs[:, 5, :], 1.0, gs[:, 6, :], ALU.add, ALU.mult)
                        dve.drain()
                        v.reciprocal(gs[:, 8, :], gs[:, 7, :])
                        dve.drain()
                        v.tensor_tensor(gs[:, 9, :], gs[:, 8, :], gs[:, 5, :], ALU.mult)
                        dve.drain()
                        v.tensor_tensor(ta[:, :, :], oh[:, 1, :, :], gs[:, 9, :].unsqueeze(2).broadcast_to([P, TT, NE]), ALU.mult)
                        dve.drain()
                        v.tensor_tensor(em[:, 0, :, :], oh[:, 0, :, :], gs[:, 8, :].unsqueeze(2).broadcast_to([P, TT, NE]), ALU.mult)
                        dve.drain()
                        v.tensor_tensor(W[:, :, 0:NE], em[:, 0, :, :], ta[:, :, :], ALU.add)
                        dve.drain()
                        last = v.tensor_tensor(sel[:, :, :], oh[:, 0, :, :], oh[:, 1, :, :], ALU.add)
                    elif kind == "rank":
                        v.tensor_copy(cnt[:, 0:1], bank[0:NE, 2 * NE:2 * NE + 1])
                        v.scalar_tensor_tensor(R[:, :, 0:NE], bank[:, 0:2 * NE].rearrange("p (t e) -> p t e", t=TT), 1.0,
                                               sel[:, :, :], ALU.add, ALU.mult)
                        over = SEQ // SLOTS - 1
                        dve.drain()
                        v.tensor_scalar(R[:, :, 0:NE], R[:, :, 0:NE], -1.0, None, ALU.add)
                        dve.drain()
                        v.tensor_scalar(cnt[:, 4:4 + over], iota[0:NE, SLOTS:SEQ:SLOTS], cnt[:, 0:1], None, ALU.is_lt)
                        dve.drain()
                        v.tensor_reduce(cnt[:, 1:2], cnt[:, 4:4 + over], AX_X, ALU.add)
                        dve.drain()
                        last = v.tensor_copy(cnt[:, 12:], cnt[:, 1:2].broadcast_to([NE, EXTRA]))
                    elif kind == "ov1":
                        v.tensor_scalar(ovd[:, 0, :], bank[0:EXTRA, 0:NE], jcol[0:EXTRA, 0:1], None, ALU.is_le)
                        dve.drain()
                        v.tensor_tensor(ovd[:, 1, :], ovd[:, 0, :], bank[0:EXTRA, NE:2 * NE], ALU.mult)
                        dve.drain()
                        v.tensor_reduce(ovv[:, 0:2], ovd[:, :, :], AX_X, ALU.add)
                        dve.drain()
                        last = v.tensor_scalar(ovv[:, 1:2], ovv[:, 1:2], -float(SLOTS), jcol[0:EXTRA, 1:2], ALU.mult, ALU.add)
                    elif kind == "ov2":
                        if True:
                            v.tensor_copy(items[0:1, 0:2 * EXTRA + 1], bank[0:1, 0:2 * EXTRA + 1])
                            v.tensor_copy(items[0:1, 2 * EXTRA + 1:2 * EXTRA + 2], prior[:, 0:1])
                            dve.drain()
                            last = v.tensor_tensor(prior[:, 0:1], prior[:, 0:1], bank[0:1, 2 * EXTRA:2 * EXTRA + 1], ALU.add)
                    last.then_inc(done["dve"], 1)

                dve.drain()
                g0 = li * (BATCHES + 1) + 1
                prep(0)
                for part in range(3):
                    prep_copy(M, 0, g0, part, P)
                with dve.Fori(0, TURNS) as turn:
                    for b in range(2):
                        for u in range(NQ):
                            e = li * NE + (turn * 2 + b) * NQ + u + 1
                            if u == 0:
                                prep(turn * 2 + b + 1)
                            activate(M, e)
                            if u < 3:
                                prep_copy(M, 1 - b, g0 + turn * 2 + b + 1, u, P)
                            y_copy(M, u, e)
                dve.drain()
                n, prev = extras(dve)
                with dve.If(n > 0):
                    with dve.Fori(0, n) as j:
                        e = prev + j + 1
                        ex, r0 = extra_item(dve, j)
                        prep_extra(ex, r0)
                        for part in range(3):
                            prep_copy(V, 0, e, part, SLOTS)
                        activate(V, e)
                        y_copy(V, 0, e)
                dve.wait_ge(M["combined"], 1 + (li + 1) * BATCHES)
                dve.wait_ge(V["combined"], 1 + prev + n)
                for h in range(2):
                    last = v.tensor_copy(x[:, 0, h * PW:(h + 1) * PW], ps[h][:, :])
                last.then_inc(sums_read_dve, 1)

            dve.wait_ge(sums_read_act, 1 + DEPTH)
            dve.drain()
            v.scalar_tensor_tensor(xh[:, 0, :], x[:, 0, :], 1.0, x[:, 0, :], ALU.mult, ALU.mult, accum_out=st2[:, 0:1])
            dve.wait_ge(final_act, 1)
            rsqrt(st2, TT, 1.0 / D).then_inc(final_dve, 1)
            dve.drain()
            dve.wait_ge(fw_loaded, 16)
            for t in range(TT):
                v.scalar_tensor_tensor(fin[:, t, :], x[:, t, :], st2[:, TT + t:TT + t + 1], fw[:, :], ALU.mult, ALU.mult
                                       ).then_inc(final_dve, 1)


def kernel(**inputs):
    import numpy as np
    import concourse.bacc as bacc
    from concourse.bass_utils import run_bass_kernel_spmd as run

    a = {k: np.asarray(v) for k, v in inputs.items()}
    col = lambda v, order: v.reshape(DEPTH, KC, P).transpose(0, 2, 1) if order == "kp" else v.reshape(DEPTH, P, KC)
    taps = a["ssd_conv_w"].reshape(DEPTH, TAPS, CC, P).transpose(0, 3, 2, 1).reshape(DEPTH, P, CC * TAPS)
    cols = np.concatenate([col(a["attn_norm_w"], "kp"), col(a["ffn_norm_w"], "pk"), taps,
                           a["ssd_conv_b"].reshape(DEPTH, CC, P).transpose(0, 2, 1)], axis=2)
    lambda_init = [0.8 - 0.6 * math.exp(-0.3 * l) for l in range(DEPTH)]
    lam = np.array([[li, 1.0 - li] for li in lambda_init], dtype=np.float32)
    flat = lambda v: v.reshape(DEPTH, -1)
    rows = np.concatenate([a["ssd_norm_w"], a["diff_subln_w"], a["ssd_d"], flat(a["ssd_dt_bias"]), flat(a["ssd_a_log"]),
                           a["swa_sink"], flat(a["diff_lambda"]), lam, a["b_router_group"], a["b_router_expert"]], axis=1)
    router = np.concatenate([a["w_router_group"], a["w_router_expert"]], axis=2)
    w_in = a["w_in"]
    aq = w_in[:, :, O_AQ:O_AK].reshape(DEPTH, D, A_KV, REP, A_D).transpose(0, 1, 3, 2, 4).reshape(DEPTH, D, A_Q)
    w_in = np.concatenate([w_in[:, :, :O_AQ], aq, w_in[:, :, O_AK:]], axis=2)
    given = {"x": a["x"], "cols": cols, "rows": rows, "w_in": w_in, "w_out": a["w_out"], "router": router,
             "w_gate": a["w_gate"], "w_up": a["w_up"], "w_down": a["w_down"], "final_w": a["final_norm_w"]}

    nc = bacc.Bacc("TRN2", target_bir_lowering=False, num_devices=1)
    arrays, args = {}, []
    for name, v in given.items():
        v = np.ascontiguousarray(v)
        arrays[f"in_{name}"] = v
        args.append(nc.dram_tensor(f"in_{name}", v.shape, mybir.dt.from_np(v.dtype), kind="ExternalInput").ap())
    args.append(nc.dram_tensor("out", (1, SEQ, D), F32, kind="ExternalOutput").ap())
    build_encoder(nc, *args)
    return run(nc, [arrays], core_ids=[0]).results[0]["out"]
```

```python
import math
from contextlib import ExitStack

import concourse.bass as bass
from concourse import mybir

ALU = mybir.AluOpType
ACT = mybir.ActivationFunctionType
AX_X = mybir.AxisListType.X
F32 = mybir.dt.float32
BF16 = mybir.dt.bfloat16
I32 = mybir.dt.int32

P = 128
DEPTH, SEQ, D = 2, 256, 1024
TT = SEQ // P
KC = D // P
EPS = 1e-6
NEG = -1e30

A_H, A_KV, A_D = 6, 2, 64
REP = A_H // A_KV
WINDOW = 128
S_H, S_P, S_N, S_G, TAPS = 6, 64, 64, 2, 5
S_IN = S_H * S_P
S_REP = S_H // S_G
C_H, C_QK, C_V = 4, 32, 64
A_Q, A_K = A_H * A_D, A_KV * A_D
S_CONV = S_IN + 2 * S_G * S_N
CC = S_CONV // P
O_AQ = 0
O_AK = O_AQ + A_Q
O_AV = O_AK + A_K
O_Z = O_AV + A_K
O_XBC = O_Z + S_IN
O_DT = O_XBC + S_CONV
O_CQ = O_DT + 2 * S_H
O_CK = O_CQ + 2 * C_H * C_QK
O_CV = O_CK + 2 * C_H * C_QK
D_IN = O_CV + C_H * C_V
D_MIX = A_Q + S_IN + C_H * C_V
MC = D_MIX // P
SLOPE = [2.0 ** (-8.0 * (i + 1) / (A_H + C_H)) for i in range(A_H + C_H)]
A_SCALE, C_SCALE = A_D ** -0.5, C_QK ** -0.5

W_IN_PIECES = [(O_XBC, 512), (O_XBC + 512, O_CK - O_XBC - 512), (O_AQ, O_AV), (O_AV, O_XBC - O_AV), (O_CK, D_IN - O_CK)]
W_OUT_PIECES = [(0, 512), (512, 512)]
PIECES = len(W_IN_PIECES) + len(W_OUT_PIECES)
PW = 512

NG, EPG = 4, 8
NE = NG * EPG
FF = 512
FC = FF // P
SLOTS = 32
NQ = P // SLOTS
GQ, DQ = FF // NQ, D // NQ
MORE = SEQ // SLOTS - 1
HALF = KC // 2
BATCHES = NE // NQ
TURNS = BATCHES // 2
TURN = 2 * NQ
GU = [0, 1, 2, 0, 1, 2, 0, 1]
GU_USES = [GU.count(c) for c in range(3)]
GU_LAST = [next(n for n in range(1, TURN + 1) if GU[(u - n) % TURN] == GU[u]) for u in range(TURN)]

K_AN, K_FN, K_CW, K_CB = 0, KC, 2 * KC, 2 * KC + CC * TAPS
NCOL = K_CB + CC
R_SN = 0
R_SL = R_SN + S_IN
R_D = R_SL + C_V
R_DTB = R_D + S_H
R_AL = R_DTB + 2 * S_H
R_SK = R_AL + 2 * S_H
R_LP = R_SK + A_H
R_LI = R_LP + 4 * C_QK
R_RB = R_LI + 2
NROW = R_RB + NG + NE


ORDER = """
    sq xn xT.0 xT.1 xT.2 xT.3 xT.4 xT.5 xT.6 xT.7 par xbc.0 conv.0 silu.0 xbc.1 xbc.2 conv.1 xbc.3 silu.1 conv.2
    conv.3 xbc.4 dt silu.2 conv.4 cq.0 xs.0 cq.1 aq.0 silu.3 dta aq.1 xs.1 lam silu.4 aq.2 cum ak cb.0 xdt cb.1 sc.0
    nm.0 row.0.0 row.0.1 sc.1 vz.0 nm.1 row.1.0 y.0 pT.0 row.1.1 row.2.0 row.2.1 sc.2 y.1 row.3.0 row.3.1 zs.0 sc.3
    pT.1 y.2 nm.2 vz.1 nm.3 y.3 row.4.0 row.4.1 sc.4 row.5.0 zs.1 row.5.1 ck.0 y.4 ck.1 nm.4 sc.5 pT.2 y.5 pT.3 sc.6
    cv nm.5 oa.0 ybn pT.4 pT.5 sc.7 oa.1 yT.0 sc.8 nm.6 yT.1 oa.2 sc.9 sc.10 nm.7 sc.11 pT.6 outA.0.0 sc.12 pT.7
    outA.0.1 nm.8 sc.13 od.0 od.1 nm.9 pT.8 outA.1.0 pT.9 od.2 od.3 ycn outA.1.1 cT outB.0.0 outB.0.1 outB.1.0
    outB.1.1 xc2.0 xc2.1 fT.0 fT.1 fT.2 fT.3 sq2 xn2 lg route rank hot ov
"""
STEPS = [(name, *map(int, index)) for name, *index in (step.split(".") for step in ORDER.split())]
ON_PE = {"xT", "xbc", "dt", "cq", "aq", "ak", "cum", "xs", "cb", "row", "sc", "y", "vz", "pT", "ck", "cv", "oa", "od",
         "yT", "cT", "outA", "outB", "fT", "lg", "rank", "ov"}
ON_DVE = {"xc2", "hot", "sq", "xn", "par", "lam", "dt", "dta", "conv", "silu", "cum", "xdt", "row", "sc", "nm", "y", "zs", "ybn", "ycn", "sq2",
          "xn2", "lg", "route", "rank", "ov"}
ON_ACT = {"sq", "xn", "par", "lam", "dta", "silu", "row", "sc", "vz", "zs", "pT", "ck", "cv", "oa", "od", "yT", "cT", "cq",
          "aq", "ak", "xs", "cb", "sq2", "xn2", "route"}


def shared(step):
    return step[0] in ("xT", "xbc", "fT")


def on(engine, step):
    if engine == "pe":
        return step[0] in ON_PE
    if shared(step):
        return (step[1] % 2 == 0) == (engine == "act")
    return step[0] in (ON_DVE if engine == "dve" else ON_ACT)


COUNT = {e: {} for e in ("pe", "act", "dve")}
for _e in COUNT:
    for _s in STEPS:
        if on(_e, _s):
            COUNT[_e][_s] = len(COUNT[_e]) + 1

LAST_USE = [("xbc", 3), ("cq", 1), ("ak",), ("vz", 1), ("cv",)]

PE_STEPS = list(COUNT["pe"])
FIRST_OUT = PE_STEPS.index(("outA", 0, 0))
BANK, HELD = {}, {}
_last, _n = {}, 0
for _i, _s in enumerate(PE_STEPS):
    if _s[0] in ("outA", "outB"):
        BANK[_s] = 2 * _s[1] + _s[2]
    elif _s[0] == "ov":
        BANK[_s] = 7
    else:
        BANK[_s] = _n % 8 if _i < FIRST_OUT else 4 + _n % 4
        _n += 1
    if BANK[_s] in _last and _s[0] != "outB":
        HELD[_s] = _last[BANK[_s]]
    _last[BANK[_s]] = _s


def reader(step):
    if shared(step):
        return "act" if step[1] % 2 == 0 else "dve"
    return "dve" if step[0] in ("dt", "cum", "sc", "y", "lg", "rank", "ov") else "act"


def build_encoder(nc, x_in, cols, rows, w_in, w_out, w_router, w_gate, w_up, w_down, final_w, out):
    with ExitStack() as ctx:
        def sem(name):
            return ctx.enter_context(nc.semaphore(name))

        base = [-(-nc.sbuf_base // 64) * 64]

        def sb(name, shape, dt=F32, at=None):
            size = math.prod(shape[1:]) * (2 if dt == BF16 else 4)
            here = at[0] if at is not None else base[0]
            t = nc.alloc_sbuf_tensor_at(name, shape, dt, offset=here)
            (at if at is not None else base)[0] = here + -(-size // 64) * 64
            return t

        x = sb("x", [P, TT, D])
        gate_up = [sb(f"gate_up{i}", [P, 2, KC * FF]) for i in range(2)]
        w_dn = [sb(f"w_dn{i}", [P, FC * D]) for i in range(2)]
        wmem = sb("wmem", [P, 2, KC, PW])
        wm = [wmem[:, i, :, :] for i in range(2)]
        gate_up.append(wmem[:, :, :, :].rearrange("p i k n -> p i (k n)"))
        wr = sb("wr", [P, KC, NG + NE])
        colp = sb("colp", [P, NCOL])
        rowp = sb("rowp", [P, NROW])
        ident = sb("ident", [P, P])
        identb = sb("identb", [P, P], BF16)
        upto = sb("upto", [P, P])
        since = sb("since", [P, P])
        before = sb("before", [P, P])
        ones = sb("ones", [P, P])
        smask = sb("smask", [P, 2, P], BF16)
        dist = sb("dist", [P, TT * P + P])
        distw = sb("distw", [P, TT * P + P])
        iota = sb("iota", [P, SEQ + SLOTS])
        tie = sb("tie", [P, NE])
        prior = sb("prior", [1, 2])
        more = sb("more", [1, 2 * NE + 1], I32)

        arena = base[0]
        m = [arena]
        xn = sb("xn", [P, TT, D], at=m)
        q = [arena]
        xdt = sb("xdt", [P, 2, TT, S_IN], at=q)
        pbuf2 = sb("pbuf2", [P, TT, SEQ], at=q)
        hT = sb("hT", [P, KC, SEQ], at=m)
        mixT = hT
        aqT = sb("aqT", [P, REP, SEQ], at=m)
        akT = sb("akT", [P, SEQ], at=m)
        cqT = sb("cqT", [P, 2, SEQ], at=m)
        ckT = sb("ckT", [P, 2, SEQ], at=m)
        q = [m[0]]
        PAD = SEQ + TAPS - 1
        xpad = sb("xpad", [P, CC, PAD], at=m)
        yb = sb("yb", [P, TT, S_IN], at=q)
        yc = sb("yc", [P, TT, C_H * C_V], at=q)
        q = [m[0]]
        xc = sb("xc", [P, CC, SEQ], at=m)
        E = [sb(f"E{i}", [P, 3, P], at=q) for i in range(2)]
        vz = sb("vz", [P, TT, PW], at=m)
        cv = sb("cv", [P, TT, C_H * C_V], at=m)
        pbuf = [sb("pbuf0", [P, TT, SEQ], at=m), sb("pbuf1", [P, TT, SEQ], at=m), pbuf2]
        ptb = [sb(f"ptb{i}", [P, TT, SEQ], at=m) for i in range(2)]
        xtok = sb("xtok", [P, TT, S_IN], at=m)
        CBs = sb("CBs", [P, S_G, TT, SEQ], at=m)
        tmp = sb("tmp", [P, S_IN], at=m)
        st = sb("st", [P, 32], at=m)
        dts = sb("dts", [P, TT, 2 * S_H], at=m)
        dta = sb("dta", [P, TT, 2 * S_H], at=m)
        sp = sb("sp", [P, 4, TT * 2 * S_H], at=m)
        cum = sb("cum", [P, TT, 3, 2 * S_H], at=m)
        den = sb("den", [P, 14, TT], at=m)
        nmx = sb("nmx", [P, 3, 14, TT], at=m)
        aneg = sb("aneg", [P, 2 * S_H], at=m)
        taps = sb("taps", [P, CC * (TAPS + 1)], at=m)
        nsink = sb("nsink", [P, A_H], at=m)
        lam = sb("lam", [P, 4], at=m)
        lpt = sb("lpt", [P, 2, C_QK], at=m)
        slw = sb("slw", [P, C_V], at=m)
        m2 = [arena]
        xh = sb("xh", [P, TT, D], at=m2)
        hT2 = sb("hT2", [P, KC, SEQ], at=m2)
        st2 = sb("st2", [P, 8], at=m2)
        fnw = sb("fnw", [P, KC], at=m2)
        lgt = sb("lgt", [P, TT, NG + NE], at=m2)
        ga = sb("ga", [P, 4, TT, NG], at=m2)
        gs = sb("gs", [P, 12, TT], at=m2)
        em = sb("em", [P, 2, TT, NE], at=m2)
        ta = sb("ta", [P, TT, NE], at=m2)
        oh = sb("oh", [P, 2, TT, NE], at=m2)
        sel = sb("sel", [P, TT, NE], at=m2)
        R = sb("R", [P, TT, NE + NQ], at=m2)
        W = sb("W", [P, TT, NE + NQ], at=m2)
        cnt = sb("cnt", [NE, 2 + MORE], at=m2)
        Pb = sb("Pb", [P, TT, P], at=m2)
        Pw = sb("Pw", [P, TT, P], at=m2)
        PwT = [sb(f"PwT{i}", [P, TT, P], at=m2) for i in range(2)]
        xg = [sb(f"xg{i}", [P, KC, P], at=m2) for i in range(2)]
        Pbx = sb("Pbx", [P, TT, SLOTS], at=m2)
        Pwx = sb("Pwx", [P, TT, SLOTS], at=m2)
        PwTx = sb("PwTx", [SLOTS, TT, P], at=m2)
        xs_x = sb("xs_x", [P, DQ], at=m2)
        xgx = sb("xgx", [P, KC, SLOTS], at=m2)
        ysbx = sb("ysbx", [SLOTS, D], at=m2)
        th = sb("th", [P, GQ], at=m2)
        gu = sb("gu", [P, GQ], at=m2)
        actv = sb("actv", [P, GQ], at=m2)
        actT = sb("actT", [P, P], at=m2)
        ysb = sb("ysb", [P, D], at=m2)
        squares = ysb
        m3 = [m2[0]]
        fw = sb("fw", [P, D], at=m3)
        fin = sb("fin", [P, TT, D], at=m3)
        assert max(m[0], m2[0], m3[0]) <= nc.sbuf_usable_end, (m[0], m2[0], m3[0], nc.sbuf_usable_end)

        ps = [ctx.enter_context(nc.psum_tensor(f"ps{i}", [P, 512], F32)) for i in range(8)]
        b_prep, b_gate, b_act, b_y = ps[4], ps[5], ps[6], ps[7]

        done = {e: sem(f"{e}_step_done") for e in ("pe", "act", "dve")}
        consts_ready, x_loaded, params_ready = sem("consts_ready"), sem("x_loaded"), sem("params_ready")
        more_cleared, ident_ready = sem("more_cleared"), sem("ident_ready")
        piece_ready = [sem("piece_ready0"), sem("piece_ready1")]
        gate_ready, up_ready = [sem(f"gate_ready{i}") for i in range(3)], [sem(f"up_ready{i}") for i in range(3)]
        down_ready = [sem(f"down_ready{i}") for i in range(2)]
        waits_passed = sem("waits_passed")
        names = ("prep_ready", "prep_mm", "prep_copied", "hidden_mm", "tanh_ready", "act_ready", "actT_mm",
                 "actT_copied", "down_mm", "y_copied_act", "y_copied_dve", "combined")
        M = {n: sem(n) for n in names}
        V = {n: sem("extra_" + n) for n in names + ("gather_mm", "gather_copied", "places_mm", "places_copied")}
        next_ready = sem("next_ready")
        sums_read_dve, sums_read_act = sem("sums_read_dve"), sem("sums_read_act")
        final_act, final_dve, fw_loaded, stored = sem("final_act"), sem("final_dve"), sem("fw_loaded"), sem("stored")

        NCONST = 21

        from_one = [*done.values(), *M.values(), *V.values(), next_ready, sums_read_dve, sums_read_act]

        def nth(li, who, *steps):
            return 1 + li * len(COUNT[who]) + max(COUNT[who][step] for step in steps)

        def piece_slot(n):
            return n % 2, (PIECES + 1 - n % 2) // 2

        def passes_before(eng, e):
            return eng.value_load(more[0:1, bass.ds(e + NE, 1)], min_val=0, max_val=DEPTH * 2 * SEQ // SLOTS)

        def extra_passes(eng, e):
            return eng.value_load(more[0:1, bass.ds(e, 1)], min_val=0, max_val=MORE)

        def half_of(xh, t, h):
            return xh[:, t, :].rearrange("p (k q) -> p k q", k=KC)[:, :, h * (P // 2):(h + 1) * (P // 2)]

        block = ctx.enter_context(nc.Block())

        @block.sync
        def _(sp_):
            x_v = x_in.rearrange("o (t p) d -> p (o t) d", p=P)
            sp_.dma_start(x[:, :, :], x_v).then_inc(x_loaded, 16)
            gate_v = w_gate.rearrange("l e (p k) f -> (l e) p (k f)", k=KC)
            up_v = w_up.rearrange("l e (p k) f -> (l e) p (k f)", k=KC)
            down_v = w_down.rearrange("l e (c p) d -> (l e) p c d", p=P)

            def load_matrix(i, ge, u):
                if i < 2:
                    src = (gate_v, up_v)[i][bass.ds(ge, 1), :, :].rearrange("o p n -> p (o n)")
                    sp_.dma_start(gate_up[GU[u]][:, i, :], src).then_inc((gate_ready, up_ready)[i][GU[u]], 16)
                else:
                    src = down_v[bass.ds(ge, 1), :, :, :].rearrange("o p c d -> p (o c) d")
                    sp_.dma_start(w_dn[u % 2][:, :].rearrange("p (c d) -> p c d", c=FC), src).then_inc(down_ready[u % 2], 16)

            freed = (M["hidden_mm"], M["hidden_mm"], M["down_mm"])
            freed_extra = (V["hidden_mm"], V["hidden_mm"], V["down_mm"])

            def load_first(li, u, i, total):
                sp_.wait_ge(freed_extra[i], 1 + total)
                sp_.sem_inc(waits_passed, 1)
                sp_.wait_ge(freed[i], 1 + li * NE)
                load_matrix(i, li * NE + u, u)

            def load_next(li, e, u, i):
                last = e - (GU_LAST[u] if i < 2 else 2)
                sp_.wait_ge(freed_extra[i], 1 + passes_before(sp_, last + 1))
                sp_.sem_inc(waits_passed, 1)
                sp_.wait_ge(freed[i], 2 + li * NE + last)
                load_matrix(i, li * NE + e, u)

            sp_.wait_ge(more_cleared, 1)
            with sp_.Fori(0, DEPTH) as li:
                def load_piece(n):
                    if n >= 2:
                        sp_.wait_ge(done["pe"], nth(li, "pe", LAST_USE[n - 2]))
                        sp_.sem_inc(waits_passed, 1)
                    src, (c0, w) = ((w_in, W_IN_PIECES[n]) if n < len(W_IN_PIECES)
                                    else (w_out, W_OUT_PIECES[n - len(W_IN_PIECES)]))
                    s, _ = piece_slot(n)
                    v = src[bass.ds(li, 1), :, c0:c0 + w].rearrange("o (k p) n -> p (o k) n", p=P)
                    sp_.dma_start(wm[s][:, :, 0:w], v).then_inc(piece_ready[s], 16)

                sp_.wait_ge(done["pe"], 1 + li * len(COUNT["pe"]))
                sp_.sem_inc(waits_passed, 1)
                sp_.wait_ge(done["dve"], 1 + li * len(COUNT["dve"]))
                sp_.sem_inc(waits_passed, 1)
                sp_.wait_ge(M["prep_mm"], 1 + li * 3 * (BATCHES + 1))
                sp_.sem_inc(waits_passed, 1)
                total = passes_before(sp_, NE)
                load_piece(0)
                sp_.dma_start(colp[:, :], cols[bass.ds(li, 1), :, :].rearrange("o p n -> p (o n)")).then_inc(params_ready, 16)
                sp_.dma_start(rowp[:, :], rows[bass.ds(li, 1), :].rearrange("o n -> (o n)").partition_broadcast(P)
                              ).then_inc(params_ready, 16)
                sp_.dma_start(wr[:, :, :], w_router[bass.ds(li, 1), :, :].rearrange("o (p k) n -> p (o k) n", k=KC)
                              ).then_inc(params_ready, 16)

                load_piece(1)
                for n in range(2, PIECES):
                    load_first(li, (n - 2) // 3, (n - 2) % 3, total)
                    load_piece(n)
                load_first(li, 1, 2, total)
                sp_.wait_ge(done["pe"], nth(li, "pe", ("outB", TT - 1, 1)))
                sp_.sem_inc(waits_passed, 1)
                for i in range(2):
                    load_matrix(i, li * NE + 2, 2)
                sp_.wait_ge(done["dve"], nth(li, "dve", ("ov",)))
                sp_.sem_inc(waits_passed, 1)
                for u, i in ((3, 0), (3, 1), (2, 2), (3, 2)):
                    load_next(li, u, u, i)
                for u in range(4, TURN):
                    for i in range(3):
                        load_next(li, u, u, i)
                with sp_.Fori(1, TURNS) as turn:
                    for u in range(TURN):
                        for i in range(3):
                            load_next(li, turn * TURN + u, u, i)
            sp_.wait_ge(sums_read_dve, 1 + DEPTH)
            sp_.wait_ge(sums_read_act, 1 + DEPTH)
            sp_.dma_start(fw[:, :], final_w.partition_broadcast(P)).then_inc(fw_loaded, 16)
            out_v = out.rearrange("o (t p) d -> p (o t) d", p=P)
            for t in range(TT):
                sp_.wait_ge(final_dve, t + 2)
                sp_.dma_start(out_v[:, t, :], fin[:, t, :]).then_inc(stored, 16)
            sp_.wait_ge(stored, 16 * TT)


        @block.gpsimd
        def _(pool):
            g = nc.gpsimd
            n = [0]

            def put(ins):
                n[0] += 1
                ins.then_inc(consts_ready, 1)

            def sync():
                pool.wait_ge(consts_ready, n[0])

            g.memset(more[:, :], 0).then_inc(more_cleared, 1)
            for signal in from_one:
                pool.sem_inc(signal, 1)
            g.memset(ident[:, :], 0.0).then_inc(ident_ready, 1)
            pool.wait_ge(ident_ready, 1)
            g.affine_select(out=ident[:, :], in_=ident[:, :], compare_op=ALU.not_equal, fill=1.0, base=0,
                            pattern=[[-1, P]], channel_multiplier=1).then_inc(ident_ready, 1)
            for t in (upto, since, before, ones):
                put(g.memset(t[:, :], 1.0))
            put(g.memset(smask[:, :, :], 0.0))
            put(g.memset(prior[:, :], 0.0))
            put(g.iota(dist[:, :], pattern=[[-1, TT * P + P]], base=P, channel_multiplier=1,
                       allow_small_or_imprecise_dtypes=True))
            put(g.iota(iota[:, :], pattern=[[1, SEQ + SLOTS]], base=0, channel_multiplier=0,
                       allow_small_or_imprecise_dtypes=True))
            put(g.iota(tie[:, :], pattern=[[-1, NE]], base=64, channel_multiplier=0,
                       allow_small_or_imprecise_dtypes=True))
            sync()
            row = [[1, P]]
            back = [[-1, P]]
            put(g.affine_select(out=upto[:, :], in_=upto[:, :], compare_op=ALU.is_ge, fill=0.0, base=0,
                                pattern=row, channel_multiplier=-1))
            put(g.affine_select(out=since[:, :], in_=since[:, :], compare_op=ALU.is_ge, fill=0.0, base=0,
                                pattern=back, channel_multiplier=1))
            put(g.affine_select(out=before[:, :], in_=before[:, :], compare_op=ALU.is_ge, fill=0.0, base=-1,
                                pattern=row, channel_multiplier=-1))
            put(g.affine_select(out=smask[:, 0, :], in_=smask[:, 0, :], compare_op=ALU.is_ge, fill=NEG, base=0,
                                pattern=row, channel_multiplier=-1))
            put(g.affine_select(out=smask[:, 1, :], in_=smask[:, 1, :], compare_op=ALU.is_ge, fill=NEG, base=0,
                                pattern=back, channel_multiplier=1))
            put(g.tensor_scalar(distw[:, :], dist[:, :], -1.0, None, ALU.mult))
            sync()
            pool.wait_ge(ident_ready, 2)
            put(g.tensor_copy(identb[:, :], ident[:, :]))
            wide, ediw = [[-1, TT * P + P]], [[1, TT * P + P]]
            put(g.affine_select(out=distw[:, :], in_=distw[:, :], compare_op=ALU.is_ge, fill=0.0, base=P,
                                pattern=wide, channel_multiplier=1))
            put(g.affine_select(out=dist[:, :], in_=dist[:, :], compare_op=ALU.is_ge, fill=0.0, base=-P,
                                pattern=ediw, channel_multiplier=-1))
            sync()
            put(g.tensor_tensor(dist[:, :], dist[:, :], distw[:, :], ALU.add))
            sync()
            put(g.affine_select(out=distw[:, :], in_=dist[:, :], compare_op=ALU.is_ge, fill=NEG, base=P + WINDOW,
                                pattern=wide, channel_multiplier=1))
            sync()
            put(g.affine_select(out=distw[:, :], in_=distw[:, :], compare_op=ALU.is_ge, fill=NEG, base=WINDOW - P,
                                pattern=ediw, channel_multiplier=-1))
            assert n[0] == NCONST


        @block.tensor
        def _(pe):
            mm, tr = nc.tensor.matmul, nc.tensor.transpose
            pe.wait_ge(ident_ready, 2)

            def prep(n, turn, part, bank, first=False):
                if part == 0:
                    pe.wait_ge(M["prep_ready"], 1 + 2 * n)
                    for t in range(TT):
                        last = tr(bank[:, t * P:(t + 1) * P], Pw[:, t, :], ident[:, :])
                else:
                    if first:
                        pe.wait_ge(M["prep_ready"], 2 * n)
                    else:
                        pe.wait_ge(M["prep_copied"], 3 * n - 2 + turn)
                    for k in range(HALF):
                        for t in range(TT):
                            c = (part - 1) * HALF + k
                            last = mm(bank[:, k * P:(k + 1) * P], xh[:, t, c * P:(c + 1) * P], Pb[:, t, :],
                                      start=(t == 0), stop=(t == TT - 1))
                last.then_inc(M["prep_mm"], 1)

            def prep_extra(n, e):
                for t in range(TT):
                    for j in range(NQ):
                        last = mm(b_prep[j * SLOTS:(j + 1) * SLOTS, 0:DQ], Pbx[:, t, :], xh[:, t, j * DQ:(j + 1) * DQ],
                                  start=(t == 0), stop=(t == TT - 1))
                last.then_inc(V["gather_mm"], 1)
                pe.wait_ge(M["y_copied_act"], 1 + e)
                pe.wait_ge(M["y_copied_dve"], 1 + e)
                for t in range(TT):
                    last = tr(b_y[0:SLOTS, t * P:(t + 1) * P], Pwx[:, t, :], ident[:, :])
                last.then_inc(V["places_mm"], 1)
                pe.wait_ge(V["gather_copied"], 1 + n)
                for h in range(DQ // P):
                    last = tr(b_prep[:, h * P:(h + 1) * P], xs_x[:, h * P:(h + 1) * P], ident[:, :])
                last.then_inc(V["prep_mm"], 1)

            def hidden(S, tokens, u, w):
                for k in range(KC):
                    for j in range(NQ):
                        o = k * FF + j * GQ
                        last = mm(b_gate[j * SLOTS:(j + 1) * SLOTS, 0:2 * GQ], tokens[:, k, u * SLOTS:(u + 1) * SLOTS],
                                  w[:, :, o:o + GQ], start=(k == 0), stop=(k == KC - 1))
                last.then_inc(S["hidden_mm"], 1)

            def act_transpose(S, n):
                pe.wait_ge(S["act_ready"], 1 + n)
                tr(b_act[:, 0:P], actv[:, :], ident[:, :]).then_inc(S["actT_mm"], 1)

            def down(S, w, n):
                pe.wait_ge(S["y_copied_act"], n)
                pe.wait_ge(S["y_copied_dve"], n)
                wv = w[:, :].rearrange("p (c d) -> p c d", c=FC)
                for c in range(FC):
                    for j in range(NQ):
                        last = mm(b_y[j * SLOTS:(j + 1) * SLOTS, 0:DQ], actT[:, c * SLOTS:(c + 1) * SLOTS],
                                  wv[:, c, j * DQ:(j + 1) * DQ], start=(c == 0), stop=(c == FC - 1))
                last.then_inc(S["down_mm"], 1)

            def combine(S, places, y, n):
                for t in range(TT):
                    for h in range(2):
                        last = mm(ps[2 * t + h][:, :], places[:, t, :], y[:, h * PW:(h + 1) * PW],
                                  start=False, stop=False, skip_group_check=True)
                last.then_inc(S["combined"], 1)

            with pe.Fori(0, DEPTH) as li:
                def piece(n):
                    s, uses = piece_slot(n)
                    pe.wait_ge(piece_ready[s], (li * uses + n // 2 + 1) * 16)
                    return wm[s]

                w_half = {}
                for s in STEPS:
                    if not on("pe", s):
                        continue
                    kind = s[0]
                    bank = ps[BANK[s]]
                    if s in HELD:
                        held = HELD[s]
                        pe.wait_ge(done[reader(held)], nth(li, reader(held), held))
                    if kind == "xT":
                        if s[1] == 0:
                            pe.wait_ge(done["act"], nth(li, "act", ("xn",)))
                            pe.wait_ge(done["dve"], nth(li, "dve", ("xn",)))
                        for t in range(TT):
                            last = tr(bank[:, t * P:(t + 1) * P], xn[:, t, s[1] * P:(s[1] + 1) * P], ident[:, :])
                    elif kind in ("xbc", "cq", "aq", "ak", "ck"):
                        if s == ("xbc", 0):
                            w = piece(0)
                            pe.wait_ge(done["act"], nth(li, "act", ("xT", KC - 2)))
                            pe.wait_ge(done["dve"], nth(li, "dve", ("xT", KC - 1)))
                        elif s == ("xbc", 4):
                            w = piece(1)
                        elif s == ("aq", 0):
                            w = piece(2)
                        elif s == ("ck", 0):
                            w = piece(4)
                        c = s[1] if len(s) > 1 else 0
                        for k in range(KC):
                            if kind == "xbc":
                                lhs = w[:, k, (c % 4) * P:(c % 4 + 1) * P]
                            elif kind == "cq":
                                o = O_CQ - (O_XBC + 512) + c * P
                                lhs = w[:, k, o:o + P]
                            elif kind == "aq":
                                lhs = w[:, k, c * P:(c + 1) * P]
                            elif kind == "ak":
                                lhs = w[:, k, O_AK:O_AK + P]
                            else:
                                lhs = w[:, k, c * P:(c + 1) * P]
                            last = mm(bank[:, 0:SEQ], lhs, hT[:, k, :], start=(k == 0), stop=(k == KC - 1))
                    elif kind == "dt":
                        o = O_DT - (O_XBC + 512)
                        for t in range(TT):
                            for k in range(KC):
                                last = mm(bank[:, t * 2 * S_H:(t + 1) * 2 * S_H], hT[:, k, t * P:(t + 1) * P],
                                          w[:, k, o:o + 2 * S_H], start=(k == 0), stop=(k == KC - 1))
                    elif kind == "vz":
                        if s[1] == 0:
                            w = piece(3)
                        t = s[1]
                        for k in range(KC):
                            last = mm(bank[:, :], hT[:, k, t * P:(t + 1) * P], w[:, k, :], start=(k == 0), stop=(k == KC - 1))
                    elif kind == "cv":
                        for t in range(TT):
                            for k in range(KC):
                                last = mm(bank[:, t * C_H * C_V:(t + 1) * C_H * C_V], hT[:, k, t * P:(t + 1) * P],
                                          w[:, k, O_CV - O_CK:D_IN - O_CK], start=(k == 0), stop=(k == KC - 1))
                    elif kind == "cum":
                        pe.wait_ge(consts_ready, NCONST)
                        pe.wait_ge(done["dve"], nth(li, "dve", ("dta",)))
                        for t in range(TT):
                            o = t * 4 * S_H
                            mm(bank[:, o:o + S_H], upto[:, :], dta[:, t, 0:S_H], start=True, stop=True)
                            mm(bank[:, o + S_H:o + 2 * S_H], since[:, :], dta[:, t, S_H:], start=True, stop=True)
                            last = mm(bank[:, o + 2 * S_H:o + 4 * S_H], ones[:, :], dta[:, t, :], start=True, stop=True)
                    elif kind == "xs":
                        pe.wait_ge(done["dve"], nth(li, "dve", ("silu", 2)))
                        t = s[1]
                        for c in range(S_IN // P):
                            last = tr(bank[:, c * P:(c + 1) * P], xc[:, c, t * P:(t + 1) * P], ident[:, :])
                    elif kind == "cb":
                        pe.wait_ge(done["dve"], nth(li, "dve", ("silu", 4)))
                        r = slice(s[1] * S_N, (s[1] + 1) * S_N)
                        for t in range(TT):
                            last = mm(bank[:, t * SEQ:(t + 1) * SEQ], xc[r, 3, t * P:(t + 1) * P], xc[r, 4, :],
                                      start=True, stop=True)
                    elif kind == "row":
                        _, h, d = s
                        tri = (upto, since)[d]
                        c = d * S_H + h
                        pe.wait_ge(done["dve"], nth(li, "dve", ("cum",)))
                        for o, t, masked in ((0, 0, True), (1, 1 - d, False), (2, 1, True)):
                            last = mm(bank[:, o * P:(o + 1) * P], dta[:, t, c:c + 1].broadcast_to([P, P]), tri[:, :],
                                      start=True, stop=not masked)
                            if masked:
                                last = mm(bank[:, o * P:(o + 1) * P], identb[:, :], smask[:, d, :], start=False, stop=True)
                    elif kind == "y":
                        h = s[1]
                        pe.wait_ge(done["dve"], nth(li, "dve", ("row", h, 1), ("xdt",)))
                        hs = slice(h * S_P, (h + 1) * S_P)
                        f, b = E[0], E[1]
                        for t, terms in ((0, ((f, 0, 0), (b, 0, 0), (b, 1, 1))), (1, ((f, 2, 1), (b, 2, 1), (f, 1, 0)))):
                            for n, (e, blk, src) in enumerate(terms):
                                last = mm(bank[:, t * S_P:(t + 1) * S_P], e[:, blk, :], xdt[:, 0 if e is f else 1, src, hs],
                                          start=(n == 0), stop=(n == 2))
                    elif kind == "sc":
                        u = s[1]
                        if u < A_H:
                            if u == 0:
                                pe.wait_ge(done["act"], nth(li, "act", ("ak",)))
                            r = slice((u // REP) * A_D, (u // REP + 1) * A_D)
                            ql, kr = aqT[r, u % REP, :], akT[r, :]
                        else:
                            h, mq = (u - A_H) // 2, (u - A_H) % 2
                            pe.wait_ge(done["act"], nth(li, "act", ("ck", h // 2)))
                            o = (2 * (h % 2) + mq) * C_QK
                            ql, kr = cqT[o:o + C_QK, h // 2, :], ckT[o:o + C_QK, h // 2, :]
                        for t in range(TT):
                            last = mm(bank[:, t * SEQ:(t + 1) * SEQ], ql[:, t * P:(t + 1) * P], kr, start=True, stop=True)
                    elif kind == "pT":
                        h = s[1]
                        pe.wait_ge(done["dve"], nth(li, "dve", ("nm", h)))
                        pb = pbuf[(h if h < A_H else A_H + 2 * (h - A_H)) % 3]
                        for kc in range(TT):
                            for t in range(TT):
                                last = tr(bank[:, kc * SEQ + t * P:kc * SEQ + (t + 1) * P], pb[:, t, kc * P:(kc + 1) * P],
                                          ident[:, :])
                    elif kind == "oa":
                        c = s[1]
                        pe.wait_ge(done["act"], nth(li, "act", ("pT", 2 * c + 1)))
                        for half in range(2):
                            h = 2 * c + half
                            for kc in range(TT):
                                g = h // REP
                                last = mm(bank[half * A_D:(half + 1) * A_D, 0:SEQ], vz[:, kc, g * A_D:(g + 1) * A_D],
                                          ptb[h % 2][:, kc, :], start=(kc == 0), stop=(kc == TT - 1))
                    elif kind == "od":
                        h = s[1]
                        pe.wait_ge(done["act"], nth(li, "act", ("pT", A_H + h)))
                        for t in range(TT):
                            for kc in range(TT):
                                last = mm(bank[:, t * C_V:(t + 1) * C_V], ptb[h % 2][:, kc, t * P:(t + 1) * P],
                                          cv[:, kc, h * C_V:(h + 1) * C_V], start=(kc == 0), stop=(kc == TT - 1))
                    elif kind == "yT":
                        pe.wait_ge(done["dve"], nth(li, "dve", ("ybn",)))
                        for c in range(S_IN // P):
                            last = tr(bank[:, c * P:(c + 1) * P], yb[:, s[1], c * P:(c + 1) * P], ident[:, :])
                    elif kind == "cT":
                        pe.wait_ge(done["dve"], nth(li, "dve", ("ycn",)))
                        for c in range(2):
                            for t in range(TT):
                                last = tr(bank[:, (c * TT + t) * P:(c * TT + t + 1) * P], yc[:, t, c * P:(c + 1) * P], ident[:, :])
                    elif kind in ("outA", "outB"):
                        _, t, half = s
                        if kind == "outA":
                            w_half[half] = piece(5 + half)
                            pe.wait_ge(done["act"], nth(li, "act", ("oa", 2), ("yT", 1)))
                            mm(bank[:, :], ident[:, :], x[:, t, half * PW:(half + 1) * PW], start=True, stop=False)
                        else:
                            pe.wait_ge(done["act"], nth(li, "act", ("cT",)))
                        for c in range(2 * REP) if kind == "outA" else range(2 * REP, MC):
                            last = mm(bank[:, :], mixT[:, c, t * P:(t + 1) * P], w_half[half][:, c, :], start=False, stop=(c == MC - 1))
                    elif kind == "fT":
                        if s[1] == 0:
                            pe.wait_ge(done["dve"], nth(li, "dve", ("xc2", 1)))
                        for a in range(2):
                            k = 2 * s[1] + a
                            for t in range(TT):
                                last = tr(bank[:, (a * TT + t) * P:(a * TT + t + 1) * P], xh[:, t, k * P:(k + 1) * P], ident[:, :])
                    elif kind == "lg":
                        pe.wait_ge(done["act"], nth(li, "act", ("fT", KC // 2 - 2)))
                        pe.wait_ge(done["dve"], nth(li, "dve", ("fT", KC // 2 - 1)))
                        pe.wait_ge(params_ready, (li + 1) * 48)
                        n = NG + NE
                        for t in range(TT):
                            for k in range(KC):
                                last = mm(bank[:, t * n:(t + 1) * n], hT2[:, k, t * P:(t + 1) * P], wr[:, k, :],
                                          start=(k == 0), stop=(k == KC - 1))
                    elif kind == "rank":
                        pe.wait_ge(done["dve"], nth(li, "dve", ("lg",)))
                        mm(bank[:, 0:NE], before[:, :], sel[:, 0, :], start=True, stop=True)
                        mm(bank[:, NE:2 * NE], ones[:, :], sel[:, 0, :], start=True, stop=False)
                        mm(bank[:, NE:2 * NE], before[:, :], sel[:, 1, :], start=False, stop=True)
                        for t in range(TT):
                            last = mm(bank[0:NE, 2 * NE:2 * NE + 1], sel[:, t, :], ones[:, 0:1], start=(t == 0), stop=(t == 1))
                    elif kind == "ov":
                        pe.wait_ge(done["dve"], nth(li, "dve", ("rank",)))
                        pe.sem_inc(waits_passed, 1)
                        mm(bank[0:1, 0:NE], cnt[:, 1:2], ident[0:NE, 0:NE], start=True, stop=True)
                        last = mm(bank[0:1, NE:2 * NE + 1], cnt[:, 1:2], before[0:NE, 0:NE + 1], start=True, stop=True)
                    last.then_inc(done["pe"], 1)

                g0 = li * (BATCHES + 1) + 1
                pe.wait_ge(done["act"], nth(li, "act", ("xn2",)))
                pe.sem_inc(waits_passed, 1)
                prep(g0, 0, 1, b_prep, first=True)
                prep(g0, 1, 2, b_gate, first=True)
                pe.wait_ge(M["prep_copied"], 3 * g0 - 1)
                prep(g0, 2, 0, b_prep)
                pe.wait_ge(done["dve"], nth(li, "dve", ("ov",)))
                pe.sem_inc(waits_passed, 1)
                with pe.Fori(0, TURNS) as turn:
                    for b in range(2):
                        g = g0 + turn * 2 + b
                        pe.wait_ge(M["prep_copied"], 1 + 3 * g)
                        for u in range(NQ):
                            place = b * NQ + u
                            e = li * NE + turn * TURN + place + 1
                            c = GU[place]
                            used = (li * TURNS + turn) * GU_USES[c] + GU[:place].count(c) + 1
                            pe.wait_ge(gate_ready[c], used * 16)
                            pe.wait_ge(up_ready[c], used * 16)
                            hidden(M, xg[b], u, gate_up[c])
                            if u < 3:
                                prep(g + 1, u, u, b_prep)
                            act_transpose(M, e)
                            n = extra_passes(pe, (turn * 2 + b) * NQ + u)
                            prev = passes_before(pe, (turn * 2 + b) * NQ + u)
                            pe.wait_ge(down_ready[u % 2], (li * (NE // 2) + turn * NQ + place // 2 + 1) * 16)
                            pe.wait_ge(M["actT_copied"], 1 + e)
                            down(M, w_dn[u % 2], e)
                            with pe.If(n > 0):
                                pe.wait_ge(M["prep_copied"], 3 * g + 1 + min(u + 1, 3))
                                pe.sem_inc(waits_passed, 1)
                                pe.wait_ge(next_ready, 1 + e)
                                pe.sem_inc(waits_passed, 1)
                                with pe.Fori(0, n) as j:
                                    i = prev + j + 1
                                    prep_extra(i, e)
                                    pe.wait_ge(V["prep_copied"], 1 + i)
                                    hidden(V, xgx, 0, gate_up[c])
                                    act_transpose(V, i)
                                    pe.wait_ge(V["actT_copied"], 1 + i)
                                    pe.wait_ge(V["places_copied"], 1 + i)
                                    down(V, w_dn[u % 2], i)
                                    pe.wait_ge(V["y_copied_act"], 1 + i)
                                    pe.wait_ge(V["y_copied_dve"], 1 + i)
                                    combine(V, PwTx, ysbx, i)
                                    pe.wait_ge(V["prep_ready"], 1 + i)
                                    pe.sem_inc(waits_passed, 1)
                        pe.wait_ge(M["y_copied_act"], 1 + e)
                        pe.wait_ge(M["y_copied_dve"], 1 + e)
                        combine(M, PwT[b], ysb, li * BATCHES + turn * 2 + b)

        @block.scalar
        def _(act):
            A = nc.scalar.activation
            act.wait_ge(x_loaded, 16)

            def act_tanh(S, n):
                act.wait_ge(S["hidden_mm"], 1 + n)
                A(th[:, :], b_gate[:, 0:GQ], ACT.Tanh, scale=0.5).then_inc(S["tanh_ready"], 1)

            def actT_copy(S, n):
                act.wait_ge(S["actT_mm"], 1 + n)
                A(actT[:, :], b_act[:, 0:P], ACT.Copy).then_inc(S["actT_copied"], 1)

            def y_copy(S, y, u, n):
                act.wait_ge(S["down_mm"], 1 + n)
                for j in range(NQ // 2):
                    last = A(y[u * SLOTS:(u + 1) * SLOTS, j * DQ:(j + 1) * DQ], b_y[j * SLOTS:(j + 1) * SLOTS, 0:DQ], ACT.Copy)
                last.then_inc(S["y_copied_act"], 1)

            with act.Fori(0, DEPTH) as li:
                act.wait_ge(sums_read_dve, 1 + li)
                act.sem_inc(waits_passed, 1)
                for s in STEPS:
                    if not on("act", s):
                        continue
                    kind = s[0]
                    bank = ps[BANK[s]] if s in BANK else None
                    act.drain()
                    if kind in ON_PE:
                        act.wait_ge(done["pe"], nth(li, "pe", s))
                    if kind == "sq":
                        last = A(xn[:, 1, :], x[:, 1, :], ACT.Square, accum_out=st[:, 1:2])
                    elif kind == "sq2":
                        for t in range(TT):
                            act.drain()
                            act.wait_ge(done["dve"], nth(li, "dve", ("xc2", t)))
                            last = A(squares[:, :], xh[:, t, :], ACT.Square, accum_out=st2[:, t:t + 1])
                    elif kind == "xn":
                        act.wait_ge(done["dve"], nth(li, "dve", ("sq",)))
                        last = A(xn[:, 0, :], x[:, 0, :], ACT.Copy, scale=st[:, 2:3])
                    elif kind == "xn2":
                        act.wait_ge(done["dve"], nth(li, "dve", ("sq2",)))
                        A(fnw[:, :], colp[:, K_FN:K_FN + KC], ACT.Copy)
                        act.wait_ge(done["pe"], nth(li, "pe", ("fT", KC // 2 - 1)))
                        last = A(xh[:, 1, :], xh[:, 1, :], ACT.Copy, scale=st2[:, 3:4])
                    elif kind == "par":
                        act.wait_ge(params_ready, (li + 1) * 48)
                        last = A(aneg[:, :], rowp[:, R_AL:R_AL + 2 * S_H], ACT.Exp)
                    elif kind == "lam":
                        act.wait_ge(done["dve"], nth(li, "dve", ("par",)))
                        last = A(lam[:, 2:4], lam[:, 0:2], ACT.Exp)
                    elif kind == "dta":
                        act.wait_ge(done["dve"], nth(li, "dve", ("dt",)))
                        last = A(sp[:, 2, :], sp[:, 1, :], ACT.Exp)
                    elif kind == "xT":
                        if s[1] == 0:
                            act.wait_ge(params_ready, (li + 1) * 48)
                        last = A(hT[:, s[1], :], bank[:, 0:SEQ], ACT.Copy, scale=colp[:, K_AN + s[1]:K_AN + s[1] + 1])
                    elif kind == "xbc":
                        last = A(xpad[:, s[1], TAPS // 2:TAPS // 2 + SEQ], bank[:, 0:SEQ], ACT.Copy)
                    elif kind == "silu":
                        act.wait_ge(done["dve"], nth(li, "dve", ("conv", s[1])))
                        if s[1] > 0:
                            act.wait_ge(done["dve"], nth(li, "dve", ("silu", s[1] - 1)))
                        last = A(tmp[:, 0:SEQ], xc[:, s[1], :], ACT.Tanh)
                    elif kind == "cq":
                        last = A(cqT[:, s[1], :], bank[:, 0:SEQ], ACT.Copy)
                    elif kind == "aq":
                        last = A(aqT[:, s[1], :], bank[:, 0:SEQ], ACT.Copy)
                    elif kind == "ak":
                        last = A(akT[:, :], bank[:, 0:SEQ], ACT.Copy)
                    elif kind == "ck":
                        last = A(ckT[:, s[1], :], bank[:, 0:SEQ], ACT.Copy)
                    elif kind == "cb":
                        last = A(CBs[:, s[1], :, :].rearrange("p a b -> p (a b)"), bank[:, :], ACT.Copy)
                    elif kind == "xs":
                        last = A(xtok[:, s[1], :], bank[:, 0:S_IN], ACT.Copy)
                    elif kind == "vz":
                        last = A(vz[:, s[1], :], bank[:, :], ACT.Copy)
                    elif kind == "cv":
                        last = A(cv[:, :, :].rearrange("p t n -> p (t n)"), bank[:, :], ACT.Copy)
                    elif kind == "zs":
                        act.wait_ge(done["dve"], nth(li, "dve", ("silu", 4))) if s[1] == 0 else act.wait_ge(done["dve"], nth(li, "dve", ("zs", 0)))
                        last = A(tmp[:, :], vz[:, s[1], A_K:], ACT.Tanh, scale=0.5)
                    elif kind == "row":
                        _, h, d = s
                        c = d * S_H + h
                        act.wait_ge(done["dve"], nth(li, "dve", ("cum",)))
                        if h == 0 and d == 0:
                            act.wait_ge(done["pe"], nth(li, "pe", ("xs", 1)))
                        if h > 0:
                            act.wait_ge(done["pe"], nth(li, "pe", ("y", h - 1)))
                        A(E[d][:, 0, :], bank[:, 0:P], ACT.Exp, bias=cum[:, 0, 0, c:c + 1])
                        A(E[d][:, 1, :], bank[:, P:2 * P], ACT.Exp, bias=cum[:, d, 2, c:c + 1])
                        last = A(E[d][:, 2, :], bank[:, 2 * P:3 * P], ACT.Exp, bias=cum[:, 1, 0, c:c + 1])
                    elif kind == "sc":
                        u = s[1]
                        act.wait_ge(done["dve"], nth(li, "dve", ("sc", u)))
                        pb = pbuf[u % 3]
                        for t in range(TT):
                            last = A(pb[:, t, :], pb[:, t, :], ACT.Exp, bias=nmx[:, 1, u, t:t + 1],
                                     scale=A_SCALE if u < A_H else C_SCALE, accum_out=den[:, u, t:t + 1])
                        if u < A_H:
                            last = A(nmx[:, 2, u, :], nmx[:, 1, u, :], ACT.Exp, bias=rowp[:, R_SK + u:R_SK + u + 1])
                    elif kind == "pT":
                        h = s[1]
                        if h >= 2:
                            if h < A_H:
                                act.wait_ge(done["pe"], nth(li, "pe", ("oa", h // 2 - 1)))
                            elif h < A_H + 2:
                                act.wait_ge(done["pe"], nth(li, "pe", ("oa", 2)))
                            else:
                                act.wait_ge(done["pe"], nth(li, "pe", ("od", h - A_H - 2)))
                        last = A(ptb[h % 2][:, :, :].rearrange("p a b -> p (a b)"), bank[:, :], ACT.Copy)
                    elif kind == "oa":
                        act.wait_ge(done["pe"], nth(li, "pe", ("cv",)))
                        last = A(mixT[:, s[1], :], bank[:, 0:SEQ], ACT.Copy)
                    elif kind == "od":
                        last = A(yc[:, :, s[1] * C_V:(s[1] + 1) * C_V],
                                 bank[:, 0:TT * C_V].rearrange("p (t v) -> p t v", t=TT), ACT.Copy)
                    elif kind == "yT":
                        last = A(mixT[:, REP:2 * REP, s[1] * P:(s[1] + 1) * P],
                                 bank[:, 0:S_IN].rearrange("p (c t) -> p c t", c=S_IN // P), ACT.Copy)
                    elif kind == "cT":
                        last = A(mixT[:, 2 * REP:MC, :].rearrange("p c t -> p (c t)"), bank[:, :], ACT.Copy)
                    elif kind == "fT":
                        for a in range(2):
                            k = 2 * s[1] + a
                            last = A(hT2[:, k, :], bank[:, a * SEQ:(a + 1) * SEQ], ACT.Copy, scale=colp[:, K_FN + k:K_FN + k + 1])
                    elif kind == "route":
                        act.wait_ge(done["dve"], nth(li, "dve", ("lg",)))
                        A(ga[:, 3, :, :], ga[:, 0, :, :], ACT.Exp)
                        last = A(gs[:, 5, :], gs[:, 4, :], ACT.Exp)
                    last.then_inc(done["act"], 1)

                act.wait_ge(done["dve"], nth(li, "dve", ("ov",)))
                act.sem_inc(waits_passed, 1)
                with act.Fori(0, BATCHES) as g:
                    for u in range(NQ):
                        e = li * NE + g * NQ + u + 1
                        act_tanh(M, e)
                        actT_copy(M, e)
                        n = extra_passes(act, g * NQ + u)
                        prev = passes_before(act, g * NQ + u)
                        y_copy(M, ysb, u, e)
                        with act.If(n > 0):
                            with act.Fori(0, n) as j:
                                i = prev + j + 1
                                act.wait_ge(V["places_mm"], 1 + i)
                                A(PwTx[:, :, :].rearrange("p t c -> p (t c)"), b_y[0:SLOTS, 0:SEQ], ACT.Copy
                                  ).then_inc(V["places_copied"], 1)
                                act_tanh(V, i)
                                actT_copy(V, i)
                                y_copy(V, ysbx, 0, i)
                total = passes_before(act, NE)
                act.wait_ge(M["combined"], 1 + (li + 1) * BATCHES)
                act.wait_ge(V["combined"], 1 + total)
                for h in range(2):
                    last = A(x[:, 1, h * PW:(h + 1) * PW], ps[2 + h][:, :], ACT.Copy)
                last.then_inc(sums_read_act, 1)
            act.drain()
            act.wait_ge(sums_read_dve, 1 + DEPTH)
            A(xh[:, 1, :], x[:, 1, :], ACT.Square, accum_out=st2[:, 1:2]).then_inc(final_act, 1)

        @block.vector
        def _(dve):
            v = nc.vector
            dve.wait_ge(x_loaded, 16)

            def rsqrt(s, n, scale):
                val, y, a, b = (s[:, i * n:(i + 1) * n] for i in range(4))
                dve.drain()
                v.tensor_scalar(val, val, scale, EPS, ALU.mult, ALU.add)
                dve.drain()
                v.tensor_scalar(a.bitcast(I32), val.bitcast(I32), 1, None, ALU.logical_shift_right)
                dve.drain()
                v.tensor_scalar(y.bitcast(I32), a.bitcast(I32), -1.0, 1597463007.0, ALU.mult, ALU.add)
                for _ in range(3):
                    dve.drain()
                    v.tensor_tensor(a, y, y, ALU.mult)
                    dve.drain()
                    v.scalar_tensor_tensor(b, a, -0.5, val, ALU.mult, ALU.mult)
                    dve.drain()
                    last = v.scalar_tensor_tensor(y, b, 1.5, y, ALU.add, ALU.mult)
                return last

            def prep(g):
                four = [P, TT, NQ, SLOTS]
                one_hot, weighted = (p[:, :, :].rearrange("p t (e s) -> p t e s", e=NQ) for p in (Pb, Pw))
                v.tensor_tensor(one_hot, iota[:, 0:SLOTS].unsqueeze(1).unsqueeze(1).broadcast_to(four),
                                R[:, :, bass.ds(g * NQ, NQ)].unsqueeze(3).broadcast_to(four), ALU.is_equal
                                ).then_inc(M["prep_ready"], 1)
                dve.drain()
                return v.tensor_tensor(weighted, one_hot, W[:, :, bass.ds(g * NQ, NQ)].unsqueeze(3).broadcast_to(four), ALU.mult
                                       ).then_inc(M["prep_ready"], 1)

            def prep_extra(e, r0, signal):
                for t in range(TT):
                    rank = R[:, t, bass.ds(e, 1)]
                    v.tensor_scalar(Pbx[:, t, :], iota[:, bass.ds(r0, SLOTS)], rank, None, ALU.is_equal)
                    last = v.tensor_scalar(Pwx[:, t, :], iota[:, bass.ds(r0, SLOTS)], rank, W[:, t, bass.ds(e, 1)],
                                           ALU.is_equal, ALU.mult)
                last.then_inc(signal, 1)

            def activate(S, n):
                dve.drain()
                dve.wait_ge(S["tanh_ready"], 1 + n)
                v.scalar_tensor_tensor(gu[:, :], th[:, :], 1.0, b_gate[:, 0:GQ], ALU.add, ALU.mult)
                dve.drain()
                v.scalar_tensor_tensor(actv[:, :], gu[:, :], 0.5, b_gate[:, GQ:2 * GQ], ALU.mult, ALU.mult).then_inc(S["act_ready"], 1)

            def prep_copy(b, n, turn, part, bank):
                dve.wait_ge(M["prep_mm"], 3 * n - 1 + turn)
                if part == 0:
                    last = v.tensor_copy(PwT[b][:, :, :].rearrange("p t c -> p (t c)"), bank[:, 0:SEQ])
                else:
                    ks = slice((part - 1) * HALF, part * HALF)
                    last = v.tensor_tensor(xg[b][:, ks, :], bank[:, :].rearrange("p (k c) -> p k c", k=HALF),
                                           fnw[:, ks].unsqueeze(2).broadcast_to([P, HALF, P]), ALU.mult)
                last.then_inc(M["prep_copied"], 1)

            def prep_copy_extra(n):
                dve.wait_ge(V["gather_mm"], 1 + n)
                v.tensor_copy(xs_x[:, :], b_prep[:, 0:DQ]).then_inc(V["gather_copied"], 1)
                dve.wait_ge(V["prep_mm"], 1 + n)
                by_half = [P, DQ // P, NQ, SLOTS]
                v.tensor_tensor(xgx[:, :, :].rearrange("p (j h) s -> p h j s", j=NQ),
                                b_prep[:, 0:DQ].rearrange("p (h j s) -> p h j s", h=DQ // P, j=NQ),
                                fnw[:, :].rearrange("p (j h) -> p h j", j=NQ).unsqueeze(3).broadcast_to(by_half), ALU.mult
                                ).then_inc(V["prep_copied"], 1)

            def y_copy(S, y, u, n):
                dve.wait_ge(S["down_mm"], 1 + n)
                for j in range(NQ // 2, NQ):
                    last = v.tensor_copy(y[u * SLOTS:(u + 1) * SLOTS, j * DQ:(j + 1) * DQ], b_y[j * SLOTS:(j + 1) * SLOTS, 0:DQ])
                last.then_inc(S["y_copied_dve"], 1)

            with dve.Fori(0, DEPTH) as li:
                dve.wait_ge(sums_read_act, 1 + li)
                dve.sem_inc(waits_passed, 1)
                for s in STEPS:
                    if not on("dve", s):
                        continue
                    kind = s[0]
                    bank = ps[BANK[s]] if s in BANK else None
                    dve.drain()
                    if kind in ON_PE:
                        dve.wait_ge(done["pe"], nth(li, "pe", s))
                    if kind == "sq":
                        v.scalar_tensor_tensor(xn[:, 0, :], x[:, 0, :], 1.0, x[:, 0, :], ALU.mult, ALU.mult,
                                               accum_out=st[:, 0:1])
                        dve.wait_ge(done["act"], nth(li, "act", ("sq",)))
                        dve.sem_inc(waits_passed, 1)
                        last = rsqrt(st, TT, 1.0 / D)
                    elif kind == "sq2":
                        dve.wait_ge(done["act"], nth(li, "act", ("sq2",)))
                        dve.sem_inc(waits_passed, 1)
                        last = rsqrt(st2, TT, 1.0 / D)
                    elif kind == "xn2":
                        dve.wait_ge(done["pe"], nth(li, "pe", ("fT", KC // 2 - 1)))
                        last = v.tensor_scalar(xh[:, 0, :], xh[:, 0, :], st2[:, 2:3], None, ALU.mult)
                    elif kind == "xc2":
                        for h in range(2):
                            dve.wait_ge(done["pe"], nth(li, "pe", ("outB", s[1], h)))
                            last = v.tensor_copy(half_of(xh, s[1], h), ps[2 * s[1] + h][:, :].rearrange("p (q k) -> p k q", k=KC))
                    elif kind == "xn":
                        last = v.tensor_scalar(xn[:, 1, :], x[:, 1, :], st[:, 3:4], None, ALU.mult)
                    elif kind == "xT":
                        if s[1] == 1:
                            dve.wait_ge(params_ready, (li + 1) * 48)
                        last = v.tensor_scalar(hT[:, s[1], :], bank[:, 0:SEQ], colp[:, K_AN + s[1]:K_AN + s[1] + 1], None, ALU.mult)
                    elif kind == "par":
                        dve.wait_ge(consts_ready, NCONST)
                        dve.wait_ge(done["act"], nth(li, "act", ("par",)))
                        v.tensor_scalar(taps[:, :], colp[:, K_CW:NCOL], 0.5, None, ALU.mult)
                        v.tensor_scalar(nsink[:, :], rowp[:, R_SK:R_SK + A_H], -1.0, None, ALU.mult)
                        v.memset(xpad[:, :, 0:TAPS // 2], 0.0)
                        v.memset(xpad[:, :, TAPS // 2 + SEQ:], 0.0)
                        v.tensor_scalar(slw[:, :], rowp[:, R_SL:R_SL + C_V], rowp[:, R_LI + 1:R_LI + 2], None, ALU.mult)
                        lp = rowp[:, R_LP:R_LP + 4 * C_QK].rearrange("p (a b d) -> p a b d", a=2, b=2)
                        v.tensor_tensor(lpt[:, :, :], lp[:, :, 0, :], lp[:, :, 1, :], ALU.mult)
                        dve.drain()
                        v.tensor_scalar(aneg[:, :], aneg[:, :], -1.0, None, ALU.mult)
                        dve.drain()
                        last = v.tensor_reduce(lam[:, 0:2], lpt[:, :, :], AX_X, ALU.add)
                    elif kind == "xbc":
                        last = v.tensor_copy(xpad[:, s[1], TAPS // 2:TAPS // 2 + SEQ], bank[:, 0:SEQ])
                    elif kind == "dt":
                        n = 2 * S_H
                        z, a, b, c = (sp[:, i, :] for i in range(4))
                        v.tensor_tensor(sp[:, 0, :].rearrange("p (t n) -> p t n", t=TT),
                                        bank[:, 0:TT * n].rearrange("p (t n) -> p t n", t=TT),
                                        rowp[:, R_DTB:R_DTB + n].unsqueeze(1).broadcast_to([P, TT, n]), ALU.add)
                        dve.drain()
                        last = v.scalar_tensor_tensor(a, z, -1.0, z, ALU.mult, ALU.min)
                    elif kind == "conv":
                        c = s[1]
                        dve.wait_ge(done["act" if c % 2 == 0 else "dve"], nth(li, "act" if c % 2 == 0 else "dve", ("xbc", c)))
                        k, kb = c * TAPS, CC * TAPS + c
                        v.tensor_scalar(xc[:, c, :], xpad[:, c, 0:SEQ], taps[:, k:k + 1], taps[:, kb:kb + 1], ALU.mult, ALU.add)
                        for j in range(1, TAPS):
                            dve.drain()
                            last = v.scalar_tensor_tensor(xc[:, c, :], xpad[:, c, j:j + SEQ],
                                                          taps[:, k + j:k + j + 1], xc[:, c, :], ALU.mult, ALU.add)
                    elif kind == "silu":
                        dve.wait_ge(done["act"], nth(li, "act", s))
                        c = s[1]
                        last = v.scalar_tensor_tensor(xc[:, c, :], tmp[:, 0:SEQ], 1.0, xc[:, c, :], ALU.add, ALU.mult)
                    elif kind == "zs":
                        dve.wait_ge(done["act"], nth(li, "act", s))
                        t = s[1]
                        last = v.scalar_tensor_tensor(vz[:, t, A_K:], tmp[:, :], 1.0, vz[:, t, A_K:], ALU.add, ALU.mult)
                    elif kind == "lam":
                        dve.wait_ge(done["act"], nth(li, "act", ("lam",)))
                        last = v.tensor_scalar(lam[:, 0:1], lam[:, 3:4], lam[:, 2:3], rowp[:, R_LI:R_LI + 1],
                                    ALU.subtract, ALU.subtract)
                    elif kind == "dta":
                        dve.wait_ge(done["act"], nth(li, "act", ("dta",)))
                        n = 2 * S_H
                        z, a, u, c = (sp[:, i, :] for i in range(4))
                        v.tensor_scalar(a, u, 2.0, None, ALU.add)
                        dve.drain()
                        v.reciprocal(a, a)
                        dve.drain()
                        v.tensor_tensor(u, u, a, ALU.mult)
                        dve.drain()
                        v.tensor_tensor(a, u, u, ALU.mult)
                        dve.drain()
                        v.tensor_scalar(c, a, 1.0 / 17, None, ALU.mult)
                        for j in (15, 13, 11, 9, 7, 5, 3):
                            dve.drain()
                            v.scalar_tensor_tensor(c, c, 1.0 / j, a, ALU.add, ALU.mult)
                        dve.drain()
                        v.scalar_tensor_tensor(c, c, 1.0, u, ALU.add, ALU.mult)
                        dve.drain()
                        v.tensor_scalar(z, z, 0.0, None, ALU.max)
                        dve.drain()
                        v.scalar_tensor_tensor(dts[:, :, :].rearrange("p t n -> p (t n)"), c, 2.0, z, ALU.mult, ALU.add)
                        dve.drain()
                        last = v.tensor_tensor(dta[:, :, :], dts[:, :, :],
                                               aneg[:, :].unsqueeze(1).broadcast_to([P, TT, n]), ALU.mult)
                    elif kind == "cum":
                        n = 2 * S_H
                        src = bank[:, 0:TT * 2 * n].rearrange("p (t k n) -> p t k n", t=TT, k=2)
                        v.tensor_scalar(cum[:, :, 0, :], src[:, :, 0, :], -1.0, None, ALU.mult)
                        v.tensor_copy(cum[:, :, 1, :], src[:, :, 1, :])
                        dve.drain()
                        last = v.tensor_tensor(cum[:, :, 2, :], cum[:, :, 1, :], cum[:, :, 0, :], ALU.add)
                    elif kind == "xdt":
                        dve.wait_ge(done["act"], nth(li, "act", ("xs", 1)))
                        for d in range(2):
                            for t in range(TT):
                                last = v.tensor_tensor(
                                    xdt[:, d, t, :].rearrange("p (h i) -> p h i", h=S_H),
                                    xtok[:, t, :].rearrange("p (h i) -> p h i", h=S_H),
                                    dts[:, t, d * S_H:(d + 1) * S_H].unsqueeze(2).broadcast_to([P, S_H, S_P]), ALU.mult)
                    elif kind == "row":
                        dve.wait_ge(done["act"], nth(li, "act", s))
                        _, h, d = s
                        g = h // S_REP
                        if h == 0 and d == 0:
                            dve.wait_ge(done["act"], nth(li, "act", ("cb", 1)))
                        e, cb = E[d], CBs[:, g, :, :]
                        ef = e[:, :, :].rearrange("p b t -> p (b t)")
                        if d == 0:
                            v.tensor_tensor(ef[:, 0:SEQ], ef[:, 0:SEQ], cb[:, 0, :], ALU.mult)
                            last = v.tensor_tensor(ef[:, SEQ:], ef[:, SEQ:], cb[:, 1, P:], ALU.mult)
                        else:
                            v.tensor_tensor(ef[:, 0:P], ef[:, 0:P], cb[:, 0, 0:P], ALU.mult)
                            last = v.tensor_tensor(ef[:, P:], ef[:, P:], cb[:, 1, :], ALU.mult)
                    elif kind == "y":
                        h = s[1]
                        hs = slice(h * S_P, (h + 1) * S_P)
                        last = v.scalar_tensor_tensor(yb[:, :, hs], xtok[:, :, hs], rowp[:, R_D + h:R_D + h + 1],
                                                      bank[:, 0:TT * S_P].rearrange("p (t i) -> p t i", t=TT), ALU.mult, ALU.add)
                    elif kind == "sc":
                        u = s[1]
                        if u >= 3:
                            w = u - 3
                            if w < A_H:
                                dve.wait_ge(done["pe"], nth(li, "pe", ("pT", w)))
                            elif (w - A_H) % 2 == 0:
                                dve.wait_ge(done["pe"], nth(li, "pe", ("pT", A_H + (w - A_H) // 2)))
                        pb = pbuf[u % 3]
                        table, slope = ((distw, SLOPE[u] / A_SCALE) if u < A_H
                                        else (dist, SLOPE[A_H + (u - A_H) // 2] / C_SCALE))
                        for t in range(TT):
                            o = P * (1 - t)
                            v.scalar_tensor_tensor(pb[:, t, :], table[:, o:o + SEQ], slope, bank[:, t * SEQ:(t + 1) * SEQ],
                                                   ALU.mult, ALU.add)
                        dve.drain()
                        v.reduce_max(nmx[:, 0, u, :], pb[:, :, :], AX_X)
                        if u < A_H:
                            dve.drain()
                            last = v.tensor_scalar(nmx[:, 1, u, :], nmx[:, 0, u, :], -A_SCALE, nsink[:, u:u + 1],
                                                   ALU.mult, ALU.min)
                        else:
                            dve.drain()
                            last = v.tensor_scalar(nmx[:, 1, u, :], nmx[:, 0, u, :], -C_SCALE, None, ALU.mult)
                    elif kind == "nm":
                        h = s[1]
                        if h < A_H:
                            u = h
                            dve.wait_ge(done["act"], nth(li, "act", ("sc", u)))
                            v.tensor_tensor(den[:, u, :], den[:, u, :], nmx[:, 2, u, :], ALU.add)
                            dve.drain()
                            v.reciprocal(den[:, u, :], den[:, u, :])
                            dve.drain()
                            for t in range(TT):
                                last = v.tensor_scalar(pbuf[u % 3][:, t, :], pbuf[u % 3][:, t, :], den[:, u, t:t + 1], None, ALU.mult)
                        else:
                            u = A_H + 2 * (h - A_H)
                            dve.wait_ge(done["act"], nth(li, "act", ("sc", u + 1)))
                            p0, p1 = pbuf[u % 3], pbuf[(u + 1) % 3]
                            v.reciprocal(den[:, u:u + 2, :], den[:, u:u + 2, :])
                            dve.drain()
                            v.tensor_scalar(den[:, u + 1, :], den[:, u + 1, :], lam[:, 0:1], None, ALU.mult)
                            for t in range(TT):
                                v.tensor_scalar(p0[:, t, :], p0[:, t, :], den[:, u, t:t + 1], None, ALU.mult)
                            dve.drain()
                            for t in range(TT):
                                last = v.scalar_tensor_tensor(p0[:, t, :], p1[:, t, :], den[:, u + 1, t:t + 1], p0[:, t, :],
                                                              ALU.mult, ALU.add)
                    elif kind == "ybn":
                        v.scalar_tensor_tensor(yb[:, :, :], yb[:, :, :], 0.5, vz[:, :, A_K:], ALU.mult, ALU.mult)
                        for t in range(TT):
                            dve.drain()
                            v.scalar_tensor_tensor(tmp[:, :], yb[:, t, :], 1.0, yb[:, t, :], ALU.mult, ALU.mult,
                                                   accum_out=st[:, t:t + 1])
                        rsqrt(st, TT, 1.0 / S_IN)
                        dve.drain()
                        for t in range(TT):
                            last = v.scalar_tensor_tensor(yb[:, t, :], yb[:, t, :], st[:, TT + t:TT + t + 1],
                                                          rowp[:, R_SN:R_SN + S_IN], ALU.mult, ALU.mult)
                    elif kind == "ycn":
                        dve.wait_ge(done["act"], nth(li, "act", ("od", C_H - 1)))
                        n = TT * C_H
                        ycf = yc[:, :, :].rearrange("p t (h i) -> p (t h) i", h=C_H)
                        sqf = xtok[:, :, :].rearrange("p t n -> p (t n)")[:, 0:n * C_V].rearrange("p (g i) -> p g i", g=n)
                        v.tensor_tensor(sqf, ycf, ycf, ALU.mult)
                        dve.drain()
                        v.tensor_reduce(st[:, 0:n], sqf, AX_X, ALU.add)
                        rsqrt(st, n, 1.0 / C_V)
                        dve.drain()
                        v.tensor_tensor(ycf, ycf, st[:, n:2 * n].unsqueeze(2).broadcast_to([P, n, C_V]), ALU.mult)
                        dve.drain()
                        last = v.tensor_tensor(ycf, ycf, slw[:, :].unsqueeze(1).broadcast_to([P, n, C_V]), ALU.mult)
                    elif kind == "fT":
                        for a in range(2):
                            k = 2 * s[1] + a
                            last = v.tensor_scalar(hT2[:, k, :], bank[:, a * SEQ:(a + 1) * SEQ],
                                                   colp[:, K_FN + k:K_FN + k + 1], None, ALU.mult)
                    elif kind == "lg":
                        n = NG + NE
                        v.memset(R[:, :, NE:], -1.0)
                        v.memset(W[:, :, NE:], 0.0)
                        for t in range(TT):
                            v.scalar_tensor_tensor(lgt[:, t, :], bank[:, t * n:(t + 1) * n], st2[:, 2 + t:3 + t],
                                                   rowp[:, R_RB:R_RB + n], ALU.mult, ALU.add)
                        L, Eq = lgt[:, :, 0:NG], lgt[:, :, NG:]

                        def first_of(one_hot, vals, top, score, key, k):
                            dve.drain()
                            v.tensor_tensor(score, vals, top.unsqueeze(2).broadcast_to([P, TT, k]), ALU.is_equal)
                            dve.drain()
                            v.tensor_tensor(score, score, tie[:, 0:k].unsqueeze(1).broadcast_to([P, TT, k]), ALU.mult)
                            dve.drain()
                            v.reduce_max(key, score, AX_X)
                            dve.drain()
                            return v.tensor_tensor(one_hot, score, key.unsqueeze(2).broadcast_to([P, TT, k]), ALU.is_equal)

                        dve.drain()
                        v.reduce_max(gs[:, 0, :], L, AX_X)
                        dve.drain()
                        v.tensor_tensor(ga[:, 0, :, :], L, gs[:, 0, :].unsqueeze(2).broadcast_to([P, TT, NG]), ALU.subtract)
                        first_of(ga[:, 2, :, :], L, gs[:, 0, :], ga[:, 1, :, :], gs[:, 1, :], NG)
                        dve.drain()
                        v.tensor_scalar(ga[:, 1, :, :], ga[:, 2, :, :], -1.0, -NEG, ALU.add, ALU.mult)
                        dve.drain()
                        v.tensor_tensor(em[:, 0, :, :].rearrange("p t (g e) -> p t g e", g=NG),
                                        Eq.rearrange("p t (g e) -> p t g e", g=NG),
                                        ga[:, 1, :, :].unsqueeze(3).broadcast_to([P, TT, NG, EPG]), ALU.add)
                        dve.drain()
                        v.reduce_max(gs[:, 2, :], em[:, 0, :, :], AX_X)
                        first_of(oh[:, 0, :, :], em[:, 0, :, :], gs[:, 2, :], ta[:, :, :], gs[:, 1, :], NE)
                        dve.drain()
                        v.scalar_tensor_tensor(em[:, 1, :, :], oh[:, 0, :, :], 3 * NEG, em[:, 0, :, :], ALU.mult, ALU.add)
                        dve.drain()
                        v.reduce_max(gs[:, 3, :], em[:, 1, :, :], AX_X)
                        dve.drain()
                        v.tensor_tensor(gs[:, 4, :], gs[:, 3, :], gs[:, 2, :], ALU.subtract)
                        first_of(oh[:, 1, :, :], em[:, 1, :, :], gs[:, 3, :], ta[:, :, :], gs[:, 1, :], NE)
                        dve.drain()
                        last = v.tensor_tensor(sel[:, :, :], oh[:, 0, :, :], oh[:, 1, :, :], ALU.add)
                    elif kind == "route":
                        dve.wait_ge(done["act"], nth(li, "act", ("route",)))
                        v.tensor_reduce(gs[:, 6, :], ga[:, 3, :, :], AX_X, ALU.add)
                        dve.drain()
                        v.scalar_tensor_tensor(gs[:, 7, :], gs[:, 5, :], 1.0, gs[:, 6, :], ALU.add, ALU.mult)
                        dve.drain()
                        v.reciprocal(gs[:, 8, :], gs[:, 7, :])
                        dve.drain()
                        v.tensor_tensor(gs[:, 9, :], gs[:, 8, :], gs[:, 5, :], ALU.mult)
                        dve.drain()
                        v.tensor_tensor(ta[:, :, :], oh[:, 1, :, :], gs[:, 9, :].unsqueeze(2).broadcast_to([P, TT, NE]), ALU.mult)
                        dve.drain()
                        v.tensor_tensor(em[:, 0, :, :], oh[:, 0, :, :], gs[:, 8, :].unsqueeze(2).broadcast_to([P, TT, NE]), ALU.mult)
                        dve.drain()
                        last = v.tensor_tensor(W[:, :, 0:NE], em[:, 0, :, :], ta[:, :, :], ALU.add)
                    elif kind == "rank":
                        v.tensor_copy(cnt[:, 0:1], bank[0:NE, 2 * NE:2 * NE + 1])
                        v.scalar_tensor_tensor(R[:, :, 0:NE], bank[:, 0:2 * NE].rearrange("p (t e) -> p t e", t=TT), 1.0,
                                               sel[:, :, :], ALU.add, ALU.mult)
                        dve.drain()
                        v.tensor_scalar(R[:, :, 0:NE], R[:, :, 0:NE], -1.0, None, ALU.add)
                        dve.drain()
                        v.tensor_scalar(cnt[:, 2:], iota[0:NE, SLOTS:SEQ:SLOTS], cnt[:, 0:1], None, ALU.is_lt)
                        dve.drain()
                        last = v.tensor_reduce(cnt[:, 1:2], cnt[:, 2:], AX_X, ALU.add)
                    elif kind == "hot":
                        prep(0)
                        last = v.memset(th[:, 0:1], 0.0)
                    elif kind == "ov":
                        v.tensor_copy(more[0:1, 0:NE], bank[0:1, 0:NE])
                        v.tensor_scalar(more[0:1, NE:], bank[0:1, NE:2 * NE + 1], prior[:, 0:1], None, ALU.add)
                        dve.drain()
                        last = v.tensor_tensor(prior[:, 0:1], prior[:, 0:1], bank[0:1, 2 * NE:2 * NE + 1], ALU.add)
                    last.then_inc(done["dve"], 1)

                dve.drain()
                g0 = li * (BATCHES + 1) + 1
                prep_copy(0, g0, 0, 1, b_prep)
                prep_copy(0, g0, 1, 2, b_gate)
                prep_copy(0, g0, 2, 0, b_prep)
                with dve.Fori(0, TURNS) as turn:
                    for b in range(2):
                        for u in range(NQ):
                            e = li * NE + (turn * 2 + b) * NQ + u + 1
                            if u == 0:
                                prep(turn * 2 + b + 1)
                            activate(M, e)
                            if u < 3:
                                prep_copy(1 - b, g0 + turn * 2 + b + 1, u, u, b_prep)
                            ex = (turn * 2 + b) * NQ + u
                            n = extra_passes(dve, ex)
                            prev = passes_before(dve, ex)
                            prep_extra(ex, SLOTS, next_ready)
                            y_copy(M, ysb, u, e)
                            with dve.If(n > 0):
                                with dve.Fori(0, n) as j:
                                    i = prev + j + 1
                                    prep_copy_extra(i)
                                    activate(V, i)
                                    y_copy(V, ysbx, 0, i)
                                    prep_extra(ex, (j + 2) * SLOTS, V["prep_ready"])
                total = passes_before(dve, NE)
                dve.wait_ge(M["combined"], 1 + (li + 1) * BATCHES)
                dve.wait_ge(V["combined"], 1 + total)
                for h in range(2):
                    last = v.tensor_copy(x[:, 0, h * PW:(h + 1) * PW], ps[h][:, :])
                last.then_inc(sums_read_dve, 1)

            dve.wait_ge(sums_read_act, 1 + DEPTH)
            dve.drain()
            v.scalar_tensor_tensor(xh[:, 0, :], x[:, 0, :], 1.0, x[:, 0, :], ALU.mult, ALU.mult, accum_out=st2[:, 0:1])
            dve.wait_ge(final_act, 1)
            rsqrt(st2, TT, 1.0 / D).then_inc(final_dve, 1)
            dve.drain()
            dve.wait_ge(fw_loaded, 16)
            for t in range(TT):
                v.scalar_tensor_tensor(fin[:, t, :], x[:, t, :], st2[:, TT + t:TT + t + 1], fw[:, :], ALU.mult, ALU.mult
                                       ).then_inc(final_dve, 1)


def kernel(**inputs):
    import numpy as np
    import concourse.bacc as bacc
    from concourse.bass_utils import run_bass_kernel_spmd as run

    a = {k: np.asarray(v) for k, v in inputs.items()}
    col = lambda v, order: v.reshape(DEPTH, KC, P).transpose(0, 2, 1) if order == "kp" else v.reshape(DEPTH, P, KC)
    taps = a["ssd_conv_w"].reshape(DEPTH, TAPS, CC, P).transpose(0, 3, 2, 1).reshape(DEPTH, P, CC * TAPS)
    cols = np.concatenate([col(a["attn_norm_w"], "kp"), col(a["ffn_norm_w"], "pk"), taps,
                           a["ssd_conv_b"].reshape(DEPTH, CC, P).transpose(0, 2, 1)], axis=2)
    lambda_init = [0.8 - 0.6 * math.exp(-0.3 * l) for l in range(DEPTH)]
    lam = np.array([[li, 1.0 - li] for li in lambda_init], dtype=np.float32)
    flat = lambda v: v.reshape(DEPTH, -1)
    rows = np.concatenate([a["ssd_norm_w"], a["diff_subln_w"], a["ssd_d"], flat(a["ssd_dt_bias"]), flat(a["ssd_a_log"]),
                           a["swa_sink"], flat(a["diff_lambda"]), lam, a["b_router_group"], a["b_router_expert"]], axis=1)
    router = np.concatenate([a["w_router_group"], a["w_router_expert"]], axis=2)
    w_in = a["w_in"]
    aq = w_in[:, :, O_AQ:O_AK].reshape(DEPTH, D, A_KV, REP, A_D).transpose(0, 1, 3, 2, 4).reshape(DEPTH, D, A_Q)
    w_in = np.concatenate([w_in[:, :, :O_AQ], aq, w_in[:, :, O_AK:]], axis=2)
    given = {"x": a["x"], "cols": cols, "rows": rows, "w_in": w_in, "w_out": a["w_out"], "router": router,
             "w_gate": a["w_gate"], "w_up": a["w_up"], "w_down": a["w_down"], "final_w": a["final_norm_w"]}

    nc = bacc.Bacc("TRN2", target_bir_lowering=False, num_devices=1)
    arrays, args = {}, []
    for name, v in given.items():
        v = np.ascontiguousarray(v)
        arrays[f"in_{name}"] = v
        args.append(nc.dram_tensor(f"in_{name}", v.shape, mybir.dt.from_np(v.dtype), kind="ExternalInput").ap())
    args.append(nc.dram_tensor("out", (1, SEQ, D), F32, kind="ExternalOutput").ap())
    build_encoder(nc, *args)
    return run(nc, [arrays], core_ids=[0]).results[0]["out"]
```
